# Optimizing a Trainium2 kernel written in Bass

```python
import jax, jax.numpy as jnp
from jax import lax
import numpy as np

D_MODEL = 1024
BATCH = 1
SEQ = 128
DEPTH = 2
DEC_BATCH = 1
DEC_SEQ = 512
PAST_LEN = 128

GRID_W = 64
N_MOD = 6
EPS = 1e-6
N_HEADS = 8
N_KV_HEADS = 2
HEAD_DIM = 64
ATTN_W = N_HEADS * HEAD_DIM
KV_W = N_KV_HEADS * HEAD_DIM
Q_BLOCK = 128
ROPE_THETA = 10000.0
HY_CH = 256
HY_GROUPS = 4
HY_SHORT = 3
HY_BANDS = 16
HY_EMB = 1 + 2 * HY_BANDS
HY_FFN = 64
HY_FILTER_STD = 0.01
HY_DECAY_MIN = 3.07
HY_DECAY_MAX = 15.35
SG_W = 256
SG_GROUPS = 4
SG_GROUP_W = SG_W // SG_GROUPS
CHUNK = 128
MIX_W = ATTN_W + HY_CH + SG_W
Q_END = ATTN_W
K_END = Q_END + KV_W
V_END = K_END + KV_W
HY_END = V_END + 3 * HY_CH
IN_W = HY_END + 2 * SG_W
PEER_HEADS = 8
N_KEYS = 128
N_EXPERTS = N_KEYS * N_KEYS
PEER_KEY_DIM = 128
PEER_HALF = PEER_KEY_DIM // 2
PEER_TOPK = 16
TOKEN_BLOCK = 128

kernel_name = 'hyena_gmlp_gqa_peer_prefix_dit_step'

F32 = jnp.float32

def rmsnorm(x, g):
    xf = x.astype(F32)
    y = xf * lax.rsqrt(jnp.mean(xf * xf, axis=-1, keepdims=True) + EPS)
    return (y * g.astype(F32)).astype(x.dtype)

def rope_2d_tables(L):
    rows = L // GRID_W
    row = jnp.broadcast_to(jnp.arange(rows, dtype=F32)[:, None], (rows, GRID_W)).reshape(L)
    col = jnp.broadcast_to(jnp.arange(GRID_W, dtype=F32)[None, :], (rows, GRID_W)).reshape(L)
    n_axis = HEAD_DIM // 4
    inv = ROPE_THETA ** (-jnp.arange(n_axis, dtype=F32) / n_axis)
    ang = jnp.concatenate([row[:, None] * inv, col[:, None] * inv], axis=-1)
    return jnp.cos(ang), jnp.sin(ang)

def apply_rope(x, cos, sin):
    B, L, H, _ = x.shape
    xp = x.astype(F32).reshape(B, L, H, HEAD_DIM // 2, 2)
    a, b = xp[..., 0], xp[..., 1]
    c = cos[None, :, None, :]
    s = sin[None, :, None, :]
    out = jnp.stack([a * c - b * s, a * s + b * c], axis=-1).reshape(B, L, H, HEAD_DIM)
    return out.astype(x.dtype)

def attention(q, k, v):
    B, Lq, H, Dh = q.shape
    G = N_HEADS // N_KV_HEADS
    nb = Lq // Q_BLOCK
    qb = q.reshape(B, nb, Q_BLOCK, N_KV_HEADS, G, Dh).transpose(1, 0, 2, 3, 4, 5)
    scale = HEAD_DIM ** -0.5

    def block(qblk):
        s = jnp.einsum('bqkgd,bskd->bkgqs', qblk, k).astype(F32) * scale
        p = jax.nn.softmax(s, axis=-1).astype(v.dtype)
        return jnp.einsum('bkgqs,bskd->bqkgd', p, v)

    o = lax.map(block, qb)
    return o.transpose(1, 0, 2, 3, 4, 5).reshape(B, Lq, H * Dh)

def short_conv(z, w, b):
    zp = jnp.pad(z, ((0, 0), (1, 1), (0, 0)))
    return zp[:, :-2] * w[0] + zp[:, 1:-1] * w[1] + zp[:, 2:] * w[2] + b

def hyena_filter_fft(L, fw1, fb1, fr1, fw2, fb2, fr2, fw3, decay):
    t = jnp.arange(L, dtype=F32)
    tn = t / (L - 1)
    w = 2.0 * jnp.pi * t / L
    f = jnp.linspace(1e-4, HY_BANDS - 1, HY_BANDS, dtype=F32)
    zf = w[:, None] * f[None, :]
    feats = jnp.concatenate([tn[:, None], jnp.cos(zf), -jnp.sin(zf)], axis=-1)
    h = jnp.sin(fr1.astype(F32) * (feats @ fw1.astype(F32) + fb1.astype(F32)))
    h = jnp.sin(fr2.astype(F32) * (h @ fw2.astype(F32) + fb2.astype(F32)))
    h = (h @ fw3.astype(F32)).reshape(L, 2, HY_CH)
    h = h * jnp.exp(-tn[:, None, None] * jnp.abs(decay.astype(F32)))
    fwd, bwd = h[:, 0], h[:, 1]
    full = jnp.concatenate([fwd, jnp.zeros((1, HY_CH), F32), bwd[:0:-1]], axis=0)
    return jnp.fft.rfft(full, axis=0)

def hyena(z, P):
    B, L, _ = z.shape
    z = short_conv(z, P['hy_conv_w'], P['hy_conv_b'])
    x0, x1, v = jnp.split(z, 3, axis=-1)
    u = (x1 * v).astype(F32)
    Hf = hyena_filter_fft(L, P['hy_fw1'], P['hy_fb1'], P['hy_freq1'], P['hy_fw2'],
                          P['hy_fb2'], P['hy_freq2'], P['hy_fw3'], P['hy_decay'])
    U = jnp.fft.rfft(u, n=2 * L, axis=1)
    conv = jnp.fft.irfft(U * Hf[None], n=2 * L, axis=1)[:, :L]
    y = x0.astype(F32) * (conv + u * P['hy_skip'].astype(F32))
    return y.astype(z.dtype)

def chunk_gmlp(z, g, ws, bs):
    B, L, _ = z.shape
    u, v = jnp.split(jax.nn.gelu(z), 2, axis=-1)
    v = rmsnorm(v, g).reshape(B, L // CHUNK, CHUNK, SG_GROUPS, SG_GROUP_W)
    v = jnp.einsum('hpq,bnqhc->bnphc', ws, v) + bs.T[None, None, :, :, None]
    return u * v.reshape(B, L, SG_W)

def peer(h, wq, keys, u_tab, v_tab):
    B, L, D = h.shape
    T = B * L
    x = h.reshape(T, D)
    q = (x @ wq).reshape(T, PEER_HEADS, 2, PEER_HALF)
    s = jnp.einsum('thpd,hpnd->thpn', q, keys).astype(F32)
    s_top, i_top = lax.top_k(s, PEER_TOPK)
    cand = (s_top[:, :, 0, :, None] + s_top[:, :, 1, None, :]).reshape(T, PEER_HEADS, PEER_TOPK * PEER_TOPK)
    cidx = (i_top[:, :, 0, :, None] * N_KEYS + i_top[:, :, 1, None, :]).reshape(T, PEER_HEADS, PEER_TOPK * PEER_TOPK)
    sc, pos = lax.top_k(cand, PEER_TOPK)
    idx = jnp.take_along_axis(cidx, pos, axis=-1)
    gate = jax.nn.softmax(sc, axis=-1)
    nb = T // TOKEN_BLOCK
    E = PEER_HEADS * PEER_TOPK
    xb = x.reshape(nb, TOKEN_BLOCK, D)
    ib = idx.reshape(nb, TOKEN_BLOCK, E)
    gb = gate.reshape(nb, TOKEN_BLOCK, E).astype(x.dtype)

    def block(args):
        xt, it, gt = args
        ue = jnp.take(u_tab, it, axis=0)
        ve = jnp.take(v_tab, it, axis=0)
        a = jax.nn.gelu(jnp.einsum('td,ted->te', xt, ue))
        return jnp.einsum('te,ted->td', gt * a, ve)

    out = lax.map(block, (xb, ib, gb))
    return out.reshape(B, L, D)

def layer(x, mod, P, rope, k_ext, v_ext):
    B, L, _ = x.shape
    sh_m, sc_m, g_m, sh_f, sc_f, g_f = jnp.split(mod, N_MOD, axis=-1)
    h = rmsnorm(x, P['norm_mix_g']) * (1.0 + sc_m) + sh_m
    proj = h @ P['w_in']
    q = rmsnorm(proj[..., :Q_END].reshape(B, L, N_HEADS, HEAD_DIM), P['q_norm_g'])
    k = rmsnorm(proj[..., Q_END:K_END].reshape(B, L, N_KV_HEADS, HEAD_DIM), P['k_norm_g'])
    v = proj[..., K_END:V_END].reshape(B, L, N_KV_HEADS, HEAD_DIM)
    if rope is None:
        attn = attention(q, k, v)
    else:
        cos, sin = rope
        q_r = apply_rope(q, cos, sin)
        k_r = apply_rope(k, cos, sin)
        k_all = jnp.concatenate([k_ext.astype(k_r.dtype), k_r], axis=1)
        v_all = jnp.concatenate([v_ext.astype(v.dtype), v], axis=1)
        attn = attention(q_r, k_all, v_all)
    hy = hyena(proj[..., V_END:HY_END], P)
    sg = chunk_gmlp(proj[..., HY_END:], P['sg_norm_g'], P['sg_w'], P['sg_b'])
    mixed = jnp.concatenate([attn, hy.astype(attn.dtype), sg.astype(attn.dtype)], axis=-1) @ P['w_out']
    x = x + g_m * mixed
    h = rmsnorm(x, P['norm_ffn_g']) * (1.0 + sc_f) + sh_f
    x = x + g_f * peer(h, P['peer_wq'], P['peer_keys'], P['peer_u'], P['peer_v'])
    return x, k, v

def setup_inputs(seed: int = 0) -> dict:
    key = jax.random.key(seed)
    ks = iter(jax.random.split(key, 40))
    D = D_MODEL

    def nrm(shape, std):
        return std * jax.random.normal(next(ks), shape, jnp.float32)

    def gain(shape):
        return 1.0 + nrm(shape, 0.02)

    return {
        'x_prompt': nrm((BATCH, SEQ, D), 1.0),
        'x_sample': nrm((DEC_BATCH, DEC_SEQ, D), 1.0),
        'cache_k': nrm((DEC_BATCH, DEPTH, PAST_LEN, N_KV_HEADS, HEAD_DIM), 1.0),
        'cache_v': nrm((DEC_BATCH, DEPTH, PAST_LEN, N_KV_HEADS, HEAD_DIM), 1.0),
        'c': nrm((DEC_BATCH, D), 1.0),
        'c_ctx': nrm((D,), 1.0),
        'norm_mix_g': gain((DEPTH, D)),
        'norm_ffn_g': gain((DEPTH, D)),
        'ada_w': nrm((DEPTH, D, N_MOD * D), D ** -0.5),
        'ada_b': nrm((DEPTH, N_MOD * D), 0.01),
        'w_in': nrm((DEPTH, D, IN_W), D ** -0.5),
        'w_out': nrm((DEPTH, MIX_W, D), MIX_W ** -0.5),
        'q_norm_g': gain((DEPTH, HEAD_DIM)),
        'k_norm_g': gain((DEPTH, HEAD_DIM)),
        'hy_conv_w': nrm((DEPTH, HY_SHORT, 3 * HY_CH), HY_SHORT ** -0.5),
        'hy_conv_b': nrm((DEPTH, 3 * HY_CH), 0.01),
        'hy_fw1': nrm((DEPTH, HY_EMB, HY_FFN), HY_EMB ** -0.5),
        'hy_fb1': nrm((DEPTH, HY_FFN), 0.1),
        'hy_freq1': 1.0 + nrm((DEPTH, HY_FFN), 0.1),
        'hy_fw2': nrm((DEPTH, HY_FFN, HY_FFN), HY_FFN ** -0.5),
        'hy_fb2': nrm((DEPTH, HY_FFN), 0.1),
        'hy_freq2': 1.0 + nrm((DEPTH, HY_FFN), 0.1),
        'hy_fw3': nrm((DEPTH, HY_FFN, 2 * HY_CH), HY_FILTER_STD),
        'hy_decay': jax.random.uniform(next(ks), (DEPTH, 2, HY_CH), jnp.float32, HY_DECAY_MIN, HY_DECAY_MAX),
        'hy_skip': nrm((DEPTH, HY_CH), 1.0),
        'sg_norm_g': gain((DEPTH, SG_W)),
        'sg_w': nrm((DEPTH, SG_GROUPS, CHUNK, CHUNK), CHUNK ** -0.5),
        'sg_b': 1.0 + nrm((DEPTH, SG_GROUPS, CHUNK), 0.02),
        'peer_wq': nrm((DEPTH, D, PEER_HEADS * PEER_KEY_DIM), D ** -0.5),
        'peer_keys': nrm((DEPTH, PEER_HEADS, 2, N_KEYS, PEER_HALF), PEER_HALF ** -0.5),
        'peer_u': nrm((DEPTH, N_EXPERTS, D), D ** -0.5),
        'peer_v': nrm((DEPTH, N_EXPERTS, D), (PEER_HEADS * PEER_TOPK) ** -0.5),
    }

def reference(x_prompt, x_sample, cache_k, cache_v, c, c_ctx, norm_mix_g, norm_ffn_g, ada_w, ada_b,
              w_in, w_out, q_norm_g, k_norm_g, hy_conv_w, hy_conv_b, hy_fw1, hy_fb1, hy_freq1,
              hy_fw2, hy_fb2, hy_freq2, hy_fw3, hy_decay, hy_skip, sg_norm_g, sg_w, sg_b,
              peer_wq, peer_keys, peer_u, peer_v):
    rope = rope_2d_tables(x_sample.shape[1])
    y_p = x_prompt
    y_s = x_sample
    ks_ctx = []
    vs_ctx = []
    for l in range(DEPTH):
        P = {
            'norm_mix_g': norm_mix_g[l], 'norm_ffn_g': norm_ffn_g[l],
            'w_in': w_in[l], 'w_out': w_out[l],
            'q_norm_g': q_norm_g[l], 'k_norm_g': k_norm_g[l],
            'hy_conv_w': hy_conv_w[l], 'hy_conv_b': hy_conv_b[l],
            'hy_fw1': hy_fw1[l], 'hy_fb1': hy_fb1[l], 'hy_freq1': hy_freq1[l],
            'hy_fw2': hy_fw2[l], 'hy_fb2': hy_fb2[l], 'hy_freq2': hy_freq2[l],
            'hy_fw3': hy_fw3[l], 'hy_decay': hy_decay[l], 'hy_skip': hy_skip[l],
            'sg_norm_g': sg_norm_g[l], 'sg_w': sg_w[l], 'sg_b': sg_b[l],
            'peer_wq': peer_wq[l], 'peer_keys': peer_keys[l],
            'peer_u': peer_u[l], 'peer_v': peer_v[l],
        }
        mod_ctx = (jax.nn.silu(c_ctx)[None, :] @ ada_w[l] + ada_b[l])[:, None, :]
        mod_lat = (jax.nn.silu(c) @ ada_w[l] + ada_b[l])[:, None, :]
        y_p, k_l, v_l = layer(y_p, mod_ctx, P, None, None, None)
        ks_ctx.append(k_l)
        vs_ctx.append(v_l)
        y_s, _, _ = layer(y_s, mod_lat, P, rope, cache_k[:, l], cache_v[:, l])
    new_cache_k = jnp.stack(ks_ctx, axis=1)
    new_cache_v = jnp.stack(vs_ctx, axis=1)
    return (y_p, y_s, new_cache_k, new_cache_v)


_drawn_inputs = setup_inputs


def setup_inputs(seed=0):
    import zlib

    import numpy as np

    out = dict(_drawn_inputs(seed))
    spreads = {}
    factors = {'cache_k': 4.287,
     'cache_v': 3.649,
     'norm_ffn_g': 8.0,
     'q_norm_g': 8.0,
     'k_norm_g': 2.785,
     'hy_conv_b': 4.611,
     'hy_freq1': 3.485,
     'hy_freq2': 2.728,
     'sg_norm_g': 8.0,
     'sg_b': 8.0}
    for name, (base, spread) in spreads.items():
        noise = np.random.default_rng([zlib.crc32(name.encode()), seed]).standard_normal(out[name].shape)
        drawn = base * np.exp(spread * noise) if base else spread * noise
        out[name] = __import__('jax').numpy.asarray(drawn.astype(out[name].dtype))
    for name, factor in factors.items():
        out[name] = (out[name] * factor).astype(out[name].dtype)
    return out
```

```python
from contextlib import ExitStack

import numpy as np

import concourse.bass as bass
from concourse import mybir

F32 = mybir.dt.float32
U32 = mybir.dt.uint32
ALU = mybir.AluOpType
ACT = mybir.ActivationFunctionType
AX = mybir.AxisListType

P = 128
D_MODEL = 1024
DEPTH = 2
LAT = 512
CTX = 128
TOK = LAT + CTX
PAST = 128
GRID_W = 64
EPS = 1e-6
HEAD_DIM = 64
ROPE_THETA = 10000.0
HY_CH = 256
HY_BANDS = 16
HY_EMB = 1 + 2 * HY_BANDS
HY_FFN = 64
SG_W = 256
PEER_HEADS = 8
N_KEYS = 128
TOPK = 16
N_EXPERTS = N_KEYS * N_KEYS

KC = D_MODEL // P
TILES = TOK // P
LAT_TILES = LAT // P
MIX_CHUNKS = 8
FREQ_CHUNKS = LAT // P
N_MOD_BLOCKS = 6 * D_MODEL // 512
BLOCK = 2048
SLOTS = 8
RING = SLOTS * BLOCK
U_SLOTS = 8
V_SLOTS = 8
UNITS = TILES * PEER_HEADS
PAD = LAT + 2 + CTX + 2
CONV = PAD - 2

S_GMIX = 0
S_GFFN = S_GMIX + KC
S_ADAB = S_GFFN + KC
S_QG = S_ADAB + 6 * KC
S_KG = S_QG + 1
S_CONVW = S_KG + 1
S_CONVB = S_CONVW + 18
S_FR1 = S_CONVB + 6
S_FB1 = S_FR1 + 1
S_FR2 = S_FB1 + 1
S_FB2 = S_FR2 + 1
S_SKIP = S_FB2 + 1
S_COLS = S_SKIP + 2

TWO_PI = 2.0 * np.pi
PI_HI = 6.28125
PI_MID = float(np.float32(TWO_PI - PI_HI))
PI_LO = float(np.float32(TWO_PI - PI_HI - PI_MID))
ROUND = 1.5 * 2.0 ** 23
SIN_MAX = 3.1415925

STREAM = ([("ada", i, ("mod_mm", i // 2 + 1)) for i in range(16)]
          + [("dft", 0, ("hf_mm", 4)), ("dft", 1, ("hf_mm", 4))]
          + [("ada", i, ("mod_mm", i // 2 + 1)) for i in range(16, 24)]
          + [("win", 0, ("vt_mm", 5)), ("win", 1, ("vt_mm", 5)), ("win", 2, ("hy_mm", 2)), ("win", 3, ("hy_mm", 4)),
             ("win", 4, ("hy_mm", 6)), ("win", 5, ("su_mm", 2)), ("win", 6, ("qk_mm", 3)), ("win", 7, ("qk_mm", 5))]
          + [("dft", 0, ("df_mm", 4)), ("dft", 1, ("df_mm", 4)), ("dft", 2, ("cv_mm", 2)), ("dft", 3, ("cv_mm", 2))]
          + [("wout", i, ("wout_mm", 2 * i + 2)) for i in range(4)]
          + [("wq", i, ("wq_mm", 2 * i + 2)) for i in range(4)]
          + [("keys", 0, ("key_mm", 2 * TILES))])
AT = {}
for _n, (_kind, _i, _) in enumerate(STREAM):
    AT.setdefault((_kind, _i), []).append(_n)


def mixer_peer_kernel(nc, xT_in, cT_in, cache_k, cache_v, ada, win, wout, wq, dft, dft_ctx, small, wide, decays,
                      fw12, featsT, sgw, keysT, rope, consts, peer_u, peer_v,
                      y_prompt, y_sample, new_k, new_v):
    with ExitStack() as ctx:
        def sb(name, cols, dt=F32, parts=P):
            return ctx.enter_context(nc.sbuf_tensor(name, [parts, cols], dt))

        def sem(name):
            return ctx.enter_context(nc.semaphore(name))

        ring = sb("ring", RING)
        xT = sb("xT", KC * TOK)[:, :].rearrange("p (k t) -> p k t", k=KC)
        mix = sb("mix", KC * TOK)[:, :].rearrange("p (k t) -> p k t", k=KC)
        SCORES = (UNITS + 1) * 2 * N_KEYS
        area = sb("area", SCORES + TILES * D_MODEL)
        hT = area[:, 0:KC * TOK].rearrange("p (k t) -> p k t", k=KC)
        at = [KC * TOK]

        def part(n):
            a = at[0]
            at[0] += n
            assert at[0] <= SCORES + TILES * D_MODEL
            return area[:, a:a + n]

        filt = part(5 * 512).rearrange("p (c r n) -> p c r n", c=5, r=2)
        gate_u = part(2 * PAD).rearrange("p (j t) -> p j t", j=2)
        kT = part(PAST + TOK)
        qT = part(4 * TOK).rearrange("p (c t) -> p c t", c=4)
        probs = part(2 * TOK).rearrange("p (b s) -> p b s", b=2)
        sgwT = part(4 * P).rearrange("p (g t) -> p g t", g=4)
        transposed = part(2 * TOK)
        probsT = transposed.rearrange("p (b s) -> p b s", b=2)
        uT = transposed.rearrange("p (t n) -> p t n", t=TILES)
        scores = area[:, 0:SCORES].rearrange("p (u h n) -> p u h n", h=2, n=N_KEYS)
        h_tok = area[:, SCORES:SCORES + TILES * D_MODEL]

        x1 = sb("x1", PAD)
        sg_v = sb("sg_v", TILES * SG_W)[:, :].rearrange("p (t n) -> p t n", t=TILES)
        v_tok = sb("v_tok", (TILES + 1) * P)[:, :].rearrange("p (t n) -> p t n", t=TILES + 1)
        rstd = sb("rstd", TOK)
        work = rstd[:, 0:512]
        zeros = sb("zeros", P)
        tmp = sb("tmp", 2 * 1024)[:, :].rearrange("p (b n) -> p b n", b=2)
        sq = sb("sq", 2 * TOK)[:, :].rearrange("p (b n) -> p b n", b=2)
        ident = sb("ident", P)
        ones = sb("ones", P)
        head_ones = sb("head_ones", P)
        swap = sb("swap", P)
        tok_const = sb("tok_const", TILES + 1 + TOPK)
        neg_time = tok_const[:, 0:TILES]
        eps = tok_const[:, TILES:TILES + 1]
        iota16 = tok_const[:, TILES + 1:TILES + 1 + TOPK]
        cos_sin = sb("cos_sin", 2 * LAT)[:, :].rearrange("p (r t) -> p r t", r=2)
        dft128 = sb("dft128", 4 * P)[:, :].rearrange("p (r t) -> p r t", r=4)
        csil = sb("csil", 2 * KC)[:, :].rearrange("p (k s) -> p k s", s=2)
        par = sb("par", S_COLS)
        widep = sb("widep", SG_W + 2 * P)
        sg_gain = widep[:, 0:SG_W]
        sg_bias = widep[:, SG_W:SG_W + 2 * P].rearrange("p (j t) -> p j t", j=2)
        modT = sb("modT", 6 * KC * 2)[:, :].rearrange("p (j s) -> p j s", s=2)
        gate_f = sb("gate_f", TILES * KC)
        SH_M, SC_M, G_M, SH_F, SC_F, G_F = range(0, 6 * KC, KC)
        small8 = sb("small8", 64)
        ssq = small8[:, 0:5]
        sg_rstd = small8[:, 8:13]
        negmax = small8[:, 16:18]
        rowsum = small8[:, 18:20]
        rinv = small8[:, 20:22]
        layer_base = small8[:, 24:25]
        topv = sb("topv", 2 * TOPK)[:, :].rearrange("p (h k) -> p h k", h=2)
        topi = sb("topi", 2 * TOPK, U32)[:, :].rearrange("p (h k) -> p h k", h=2)
        topf = sb("topf", 2 * TOPK)[:, :].rearrange("p (h k) -> p h k", h=2)
        best = sb("best", TOPK)
        pos = sb("pos", TOPK, U32)
        posij = sb("posij", 2 * TOPK, U32)[:, :].rearrange("p (h k) -> p h k", h=2)
        posf = sb("posf", 2 * TOPK)[:, :].rearrange("p (h k) -> p h k", h=2)
        picked = sb("picked", 2 * TOPK)[:, :].rearrange("p (h k) -> p h k", h=2)
        idxf = sb("idxf", TOPK)
        idx_all = sb("idx_all", (UNITS + 1) * TOPK, U32)
        idx = [sb(f"idx{b}", TOPK, U32) for b in range(2)]
        gate_e = sb("gate_e", TOPK)
        gate_s = sb("gate_s", 4)
        dots = sb("dots", TOPK)
        acts = sb("acts", TOPK)
        wts = sb("wts", TOPK)
        unit_s = sq[:, 0, 0:2 * N_KEYS].rearrange("p (h n) -> p h n", h=2)
        cand = sq[:, 1, 0:TOPK * TOPK]
        onehot = x1[:, 0:TOPK * TOPK]
        diag = sg_v.rearrange("p t n -> p (t n)")[:, 0:4 * P].rearrange("p (b n) -> p b n", b=4)
        out_tok = tmp[:, 0, :]
        mod_row = sg_v.rearrange("p t n -> p (t n)")[:, 0:1024].rearrange("p (b n) -> p b n", b=2)
        sin_arg = probs
        sin_out = probsT
        envelope = tmp[:, :, 0:512]
        q_area = qT.rearrange("p c t -> p (c t)")
        feats, fw, decay = q_area[:, 0:TOK], q_area[:, TOK:TOK + 2 * HY_FFN + 512], q_area[:, 2 * TOK:2 * TOK + 512]
        mix_cols = mix.rearrange("p k t -> p (k t)")
        filt_ab = mix_cols[:, 0:5 * 512].rearrange("p (t r n) -> p t r n", t=5, r=2)
        x0 = mix_cols[:, 0:2 * PAD].rearrange("p (j t) -> p j t", j=2)
        raw = mix_cols[:, 2 * PAD:4 * PAD].rearrange("p (j t) -> p j t", j=2)
        k_past = tmp[:, 1, TOK:TOK + P]
        k_out = tmp[:, 1, TOK + P:TOK + 2 * P]
        sg_junk = tmp[:, 0, TOK:TOK + SG_W]
        psum = ctx.enter_context(nc.psum_tensor("psum", [P, 4, 1024], F32))

        def slot(n):
            return ring[:, (n % SLOTS) * BLOCK:(n % SLOTS + 1) * BLOCK]

        def uslot(k):
            return ring[:, (k % U_SLOTS) * D_MODEL:(k % U_SLOTS + 1) * D_MODEL]

        def vslot(k):
            a = U_SLOTS * D_MODEL + (k % V_SLOTS) * D_MODEL
            return ring[:, a:a + D_MODEL]

        const_loaded = sem("const_loaded")
        silu_ready = sem("silu_ready")
        zero_ready = sem("zero_ready")
        layer_done = sem("layer_done")
        layer_go = sem("layer_go")
        pool_tick = sem("pool_tick")
        dve_tick = sem("dve_tick")
        sp_tick = sem("sp_tick")
        names = """small_loaded cache_loaded cache_stored
        sq_ready sq_used stat_read rstd_ready xn_ready h_ready
        mod_mm modrow_ready modT_mm mod_ready scale_ready
        filt_mm arg_ready sin_ready env_ready ab_ready hf_mm filt_ready
        qk_mm hsq_ready qg_ready hs_mm hs_read hr_ready qn_ready rot_mm qk_ready
        vt_mm vt_read sgr_ready sgn_ready su_mm su_ready sp_mm sp_ready
        hy_mm hy_read hy_conv gu_ready ut_mm ut_ready df_mm y_ready cv_mm cv_ready
        ck_mm ck_ready ko_mm ko_ready
        sc_mm max_ready exp_ready probs_ready pt_mm pt_ready pv_mm attn_ready
        wout_mm x_ready wq_mm pq_ready tok_mm tok_ready key_mm key0_read key1_read
        staged idx_ready best_ready gexp_ready
        u_free gelu_ready w_ready diag_ready v_free acc_mm acc_read back_mm x_added
        dve_link act_link pads_ready wlink idx_copied topk_link""".split()
        s = {n: sem(n) for n in names}
        landed = [sem(f"landed{k}") for k in range(SLOTS)]
        u_landed = [sem(f"u_landed{k}") for k in range(U_SLOTS)]
        v_landed = [sem(f"v_landed{k}") for k in range(V_SLOTS)]
        of_layer = [pool_tick, dve_tick, *s.values(), *landed]
        y_mm, y_copied, y_stored = sem("y_mm"), sem("y_copied"), [sem("y_stored0"), sem("y_stored1")]

        ORDER = [("rms", 0)]
        ORDER += [x for n in range(6) for x in ([("mod", n)] + ([("modT", n - 1)] if n else []))]
        ORDER += [("f1", 0), ("mod", 6), ("modT", 5), ("f2", 0), ("mod", 7), ("modT", 6)]
        ORDER += [("f3", t) for t in range(TILES)] + [("hf", c) for c in range(5)]
        ORDER += [x for n in range(8, 12) for x in (("mod", n), ("modT", n - 1))] + [("modT", 11)]
        ORDER += [("qk", 0), ("vt", 0), ("hs", 0), ("vt", 1), ("vt", 2), ("rot", 0), ("vt", 3), ("vt", 4)]
        ORDER += [("hy", 0), ("ck", 0), ("hy", 1), ("ko", 0), ("hy", 2), ("hy", 3), ("hy", 4), ("hy", 5)]
        ORDER += [("su", 0), ("ut", 0), ("su", 1), ("ut", 1)]
        ORDER += [("qk", 1), ("sp", 0), ("hs", 1), ("qk", 2), ("rot", 1), ("hs", 2), ("qk", 3), ("rot", 2),
                  ("hs", 3), ("qk", 4), ("rot", 3), ("hs", 4), ("sp", 1), ("df", 0), ("rot", 4)]
        ORDER += [("df", c) for c in range(1, 5)] + [("cv", 0), ("cv", 1)]
        READ = {
            "rms": lambda n: [("stat_read", 1)], "mod": lambda n: [("modrow_ready", n + 1)],
            "modT": lambda n: [("mod_ready", n + 1)], "f1": lambda n: [("arg_ready", 1)],
            "f2": lambda n: [("arg_ready", 2)], "f3": lambda n: [("ab_ready", n + 1)],
            "hf": lambda n: [("filt_ready", n + 1)], "qk": lambda n: [("qg_ready", n + 1)],
            "vt": lambda n: [("vt_read", n + 1)], "hs": lambda n: [("hs_read", n + 1)],
            "rot": lambda n: [("qk_ready", n + 1)], "hy": lambda n: [("hy_read", n + 1)],
            "ck": lambda n: [("ck_ready", 1)], "ko": lambda n: [("ko_ready", 1)],
            "su": lambda n: [("su_ready", n + 1)], "ut": lambda n: [("ut_ready", n + 1)],
            "sp": lambda n: [("sp_ready", n + 1)], "df": lambda n: [("y_ready", n + 1)],
            "cv": lambda n: [("cv_ready", n + 1)],
        }

        def pair(*job):
            return psum[:, ORDER.index(job) % 4, :]

        def qk_dst(n):
            return kT[:, PAST:PAST + TOK] if n == 0 else qT[:, n - 1, :]

        ATT_UNITS = 40

        def unit_of(n):
            c, half, t = n // 10, n // 5 % 2, n % 5
            width = TOK if t < LAT_TILES else CTX
            return c, slice(64 * half, 64 * half + 64), t, width

        HY_CHUNK = (2, 4, 3, 5, 0, 1)

        def hy_dst(i):
            return (x1[:], gate_u[:, 0, :], x1[:], gate_u[:, 1, :], x0[:, 0, :], x0[:, 1, :])[i]

        PIECES = ((0, 0, LAT), (LAT, LAT + 2, CTX))
        TOPK_LINKS = 27
        STEPS_BEFORE_PLAIN = (10, *range(16, TOPK_LINKS + 1))
        block = ctx.enter_context(nc.Block())

        @block.sync
        def _(sp):
            for dst, src in ((xT, xT_in), (csil, cT_in), (ident[:], consts[0]), (ones[:], consts[1]),
                             (head_ones[:], consts[2]), (swap[:], consts[3]), (cos_sin, rope), (dft128, dft_ctx),
                             (tok_const[:], consts[4][:, 0:TILES + 1 + TOPK])):
                sp.dma_start(dst, src).then_inc(const_loaded, 16)
            with sp.Fori(0, DEPTH) as l:
                def of(x):
                    return x[bass.ds(l, 1)].squeeze(0)

                for dst, src in ((par[:], small), (widep[:], wide), (decay, decays), (fw[0:HY_FFN, :], fw12), (sgwT, sgw)):
                    sp.dma_start(dst, of(src)).then_inc(s["small_loaded"], 16)
                sp.dma_start(feats[0:HY_EMB, :], featsT).then_inc(s["small_loaded"], 16)
                sp.dma_start(k_past, of(cache_k)).then_inc(s["cache_loaded"], 16)
                sp.dma_start(v_tok[:, TILES, :], of(cache_v)).then_inc(s["cache_loaded"], 16)
                for n, (kind, i, _) in enumerate(STREAM):
                    if n >= SLOTS:
                        name, value = STREAM[n - SLOTS][2]
                        sp.wait_ge(s[name], value)
                    if kind == "keys":
                        sp.dma_start(slot(n)[:, 0:PEER_HEADS * N_KEYS], of(keysT)).then_inc(landed[n % SLOTS], 16)
                    else:
                        src = dft[i] if kind == "dft" else of({"ada": ada, "win": win, "wout": wout, "wq": wq}[kind])[i]
                        sp.dma_start(slot(n), src).then_inc(landed[n % SLOTS], 16)
                    if (kind, i) == ("wout", 0):
                        sp.wait_ge(s["ko_ready"], 1)
                        sp.dma_start(of(new_k), k_out).then_inc(s["cache_stored"], 16)
                        sp.wait_ge(s["vt_read"], TILES)
                        sp.dma_start(of(new_v), v_tok[:, LAT_TILES, :]).then_inc(s["cache_stored"], 16)
                sp.wait_ge(s["cache_stored"], 32)
                sp.wait_ge(layer_done, 4 * l + 4)
                sp.sem_inc(sp_tick, 1)
                for x in of_layer:
                    sp.sem_clear(x)
                sp.sem_inc(layer_go, 1)
            for t in range(TILES):
                sp.wait_ge(y_copied, t + 1)
                dst = y_sample[t * P:(t + 1) * P, :] if t < LAT_TILES else y_prompt
                sp.dma_start(dst, tmp[:, t % 2, :]).then_inc(y_stored[t % 2], 16)
            sp.wait_ge(y_stored[0], 16 * 3)
            sp.wait_ge(y_stored[1], 16 * 2)

        @block.gpsimd
        def _(pool):
            def fetch(u, table, idx, place, free, arrived):
                for k in range(TOPK):
                    pool.wait_ge(s[free], TOPK * u + k + 1)
                    pool.sem_inc(pool_tick, 1)
                    pool.indirect_dma_start(place(k), None, table,
                                            bass.IndirectOffsetOnAxis(ap=idx[:, k:k + 1], axis=0)
                                            ).then_inc(arrived[k % 8], 16)

            with pool.Fori(0, DEPTH) as l:
                pool.sem_inc(s["u_free"], U_SLOTS)
                pool.sem_inc(s["v_free"], V_SLOTS)
                with pool.Fori(0, UNITS // 2) as pair_of:
                    for b in range(2):
                        u = pair_of * 2 + b
                        pool.wait_ge(s["idx_ready"], u + 1)
                        pool.sem_inc(pool_tick, 1)
                        pool.tensor_copy(idx[b][:], idx_all[:, bass.ds(u * TOPK, TOPK)]).then_inc(s["idx_copied"], 1)
                        pool.wait_ge(s["idx_copied"], u + 1)
                        fetch(u, peer_u, idx[b], uslot, "u_free", u_landed)
                        fetch(u, peer_v, idx[b], vslot, "v_free", v_landed)
                for k in range(V_SLOTS):
                    pool.wait_ge(v_landed[k], 32 * (UNITS * l + UNITS))
                pool.sem_inc(layer_done, 1)
                pool.wait_ge(layer_go, l + 1)

        @block.tensor
        def _(pe):
            def blk(kind, i, again=0):
                n = AT[kind, i][again]
                pe.wait_ge(landed[n % SLOTS], 16 * (n // SLOTS + 1))
                return slot(n)

            def mm2(dst, lhsT, src, start, stop):
                pe.matmul(dst[:, 0:LAT], lhsT, src[:, 0:LAT], start=start, stop=stop)
                return pe.matmul(dst[:, LAT:TOK], lhsT, src[:, LAT:TOK], start=start, stop=stop)

            def rms(i, g):
                for k in range(KC):
                    pe.wait_ge(s["sq_ready"], KC * i + k + 1)
                    mm2(g, ones[:], sq[:, k % 2, :], k == 0, k == KC - 1).then_inc(s["sq_used"], 1)

            def mod(n, g):
                for half in range(2):
                    w = blk("ada", 2 * n + half)
                    for j in range(4):
                        m = pe.matmul(g[0:2, 0:512], csil[:, 4 * half + j, :], w[:, j * 512:(j + 1) * 512],
                                      start=(half == 0 and j == 0), stop=(half == 1 and j == 3))
                m.then_inc(s["mod_mm"], 1)

            def modT(n, g):
                pe.wait_ge(s["modrow_ready"], n + 1)
                for j in range(4):
                    m = pe.transpose(g[:, 2 * j:2 * j + 2], mod_row[0:2, n % 2, j * P:(j + 1) * P], ident[0:2, 0:2])
                m.then_inc(s["modT_mm"], 1)

            def f1(n, g):
                mm2(g[0:HY_FFN], fw[0:HY_EMB, 0:HY_FFN], feats[0:HY_EMB, :], True, True).then_inc(s["filt_mm"], 1)

            def f2(n, g):
                pe.wait_ge(s["sin_ready"], 1)
                mm2(g[0:HY_FFN], fw[0:HY_FFN, HY_FFN:2 * HY_FFN], sin_out[0:HY_FFN, 0, :], True, True).then_inc(s["filt_mm"], 1)

            def f3(t, g):
                pe.wait_ge(s["sin_ready"], 2)
                pe.matmul(g[:, 0:512], sin_out[0:HY_FFN, 1, t * P:(t + 1) * P], fw[0:HY_FFN, 2 * HY_FFN:],
                          start=True, stop=True).then_inc(s["filt_mm"], 1)

            def spectrum(c, g, src, again):
                for r in range(2):
                    out = g[:, r * HY_CH:(r + 1) * HY_CH]
                    if c == LAT_TILES:
                        m = pe.matmul(out, dft128[:, r, :], src(LAT_TILES, r), start=True, stop=True)
                    else:
                        w = blk("dft", r, again)
                        for t in range(LAT_TILES):
                            m = pe.matmul(out, w[:, t * LAT + c * P:t * LAT + (c + 1) * P], src(t, r),
                                          start=(t == 0), stop=(t == LAT_TILES - 1))
                return m

            def hf(c, g):
                pe.wait_ge(s["ab_ready"], TILES)
                spectrum(c, g, lambda t, r: filt_ab[:, t, r, :], 0).then_inc(s["hf_mm"], 1)

            def project(w, g, src, done, ready=None, first=0):
                for k in range(KC):
                    if ready:
                        pe.wait_ge(s[ready], first + k + 1)
                    m = mm2(g, w[:, k * P:(k + 1) * P], src[:, k, :], k == 0, k == KC - 1)
                m.then_inc(s[done], 1)

            def half_of(w, half):
                return w[:, half * 1024:(half + 1) * 1024]

            def qk(n, g):
                w = half_of(blk("win", 0), 0) if n == 0 else half_of(blk("win", 6 + (n - 1) // 2), (n - 1) % 2)
                project(w, g, hT, "qk_mm", "h_ready")

            def vt(t, g):
                blk("win", 0)
                blk("win", 1)
                a = AT["win", 0][0] % SLOTS * BLOCK + 1024
                w = ring[:, a:a + 3072].rearrange("p (c k n) -> p c k n", c=3, k=KC)
                for k in range(KC):
                    m = pe.matmul(g[:, 0:384], hT[:, k, t * P:(t + 1) * P], w[:, :, k, :], start=(k == 0), stop=(k == KC - 1))
                m.then_inc(s["vt_mm"], 1)

            def hs(n, g):
                pe.wait_ge(s["hsq_ready"], n + 1)
                mm2(g, head_ones[:], sq[:, n % 2, :], True, True).then_inc(s["hs_mm"], 1)

            def rot(n, g):
                pe.wait_ge(s["qn_ready"], n + 1)
                pe.matmul(g[:, 0:LAT], swap[:], qk_dst(n)[:, 0:LAT], start=True, stop=True).then_inc(s["rot_mm"], 1)

            def ck(n, g):
                pe.wait_ge(s["cache_loaded"], 32)
                pe.transpose(g[:, 0:P], k_past, ident[:]).then_inc(s["ck_mm"], 1)

            def ko(n, g):
                pe.wait_ge(s["qn_ready"], 1)
                pe.transpose(g[:, 0:P], kT[:, PAST + LAT:PAST + TOK], ident[:]).then_inc(s["ko_mm"], 1)

            def hy(i, g):
                project(half_of(blk("win", 2 + i // 2), i % 2), g, hT, "hy_mm")

            def su(j, g):
                project(half_of(blk("win", 5), j), g, hT, "su_mm")

            def ut(n, g):
                pe.wait_ge(s["gu_ready"], 2)
                for i, t in enumerate(range(LAT_TILES) if n == 0 else (LAT_TILES,)):
                    a = t * P if t < LAT_TILES else LAT + 2
                    for j in range(2):
                        m = pe.transpose(g[:, (2 * i + j) * P:(2 * i + j + 1) * P], gate_u[:, j, a:a + P], ident[:])
                m.then_inc(s["ut_mm"], 1)

            def sp_(j, g):
                pe.wait_ge(s["sgn_ready"], TILES)
                for t in range(TILES):
                    for half in range(2):
                        m = pe.matmul(g[64 * half:64 * half + 64, t * P:(t + 1) * P],
                                      sg_v[:, t, j * P + 64 * half:j * P + 64 * half + 64], sgwT[:, 2 * j + half, :],
                                      start=True, stop=True)
                m.then_inc(s["sp_mm"], 1)

            def df(c, g):
                pe.wait_ge(s["ut_ready"], 2)
                spectrum(c, g, lambda t, r: uT[:, t, :], 1).then_inc(s["df_mm"], 1)

            def cv(j, g):
                pe.wait_ge(s["y_ready"], 5)
                ws = [blk("dft", 2 + r) for r in range(2)]
                for c in range(FREQ_CHUNKS):
                    for r in range(2):
                        pe.matmul(g[:, 0:LAT], filt[:, c, r, j * P:(j + 1) * P], ws[r][:, c * LAT:(c + 1) * LAT],
                                  start=(c == 0 and r == 0), stop=(c == FREQ_CHUNKS - 1 and r == 1))
                for r in range(2):
                    m = pe.matmul(g[:, LAT:TOK], filt[:, FREQ_CHUNKS, r, j * P:(j + 1) * P], dft128[:, 2 + r, :],
                                  start=(r == 0), stop=(r == 1))
                m.then_inc(s["cv_mm"], 1)

            jobs = {"rms": rms, "mod": mod, "modT": modT, "f1": f1, "f2": f2, "f3": f3, "hf": hf, "qk": qk, "vt": vt,
                    "hs": hs, "rot": rot, "ck": ck, "ko": ko, "hy": hy, "su": su, "ut": ut, "sp": sp_, "df": df, "cv": cv}

            def att_scores(n):
                c, rows, t, width = unit_of(n)
                if n >= 2:
                    pe.wait_ge(s["exp_ready"], n - 1)
                g = psum[:, n % 2, :]
                q = qT[rows, c, t * P:(t + 1) * P]
                if t < LAT_TILES:
                    pe.matmul(g[:, 0:512], q, kT[rows, 0:512], start=True, stop=True)
                    m = pe.matmul(g[:, 512:TOK], q, kT[rows, 512:TOK], start=True, stop=True)
                else:
                    m = pe.matmul(g[:, 0:CTX], q, kT[rows, TOK:TOK + CTX], start=True, stop=True)
                m.then_inc(s["sc_mm"], 1)

            def att_transpose(n):
                width = unit_of(n)[3]
                pe.wait_ge(s["probs_ready"], n + 1)
                if n >= 1:
                    pe.wait_ge(s["pt_ready"], n)
                for b in range(width // P):
                    m = pe.transpose(psum[:, 2, b * P:(b + 1) * P], probs[:, n % 2, b * P:(b + 1) * P], ident[:])
                m.then_inc(s["pt_mm"], 1)

            def att_values(n):
                c, rows, t, width = unit_of(n)
                pe.wait_ge(s["pt_ready"], n + 1)
                if n % 10 == 0 and n:
                    pe.wait_ge(s["attn_ready"], n // 10)
                blocks = [TILES, 0, 1, 2, 3] if t < LAT_TILES else [LAT_TILES]
                for i, b in enumerate(blocks):
                    m = pe.matmul(psum[rows, 3, t * P:(t + 1) * P], v_tok[:, b, rows], probsT[:, n % 2, i * P:(i + 1) * P],
                                  start=(i == 0), stop=(i == len(blocks) - 1))
                m.then_inc(s["pv_mm"], 1)

            pe.wait_ge(const_loaded, 144)
            pe.wait_ge(silu_ready, 1)
            pe.wait_ge(zero_ready, 1)
            with pe.Fori(0, DEPTH) as l:
                pe.wait_ge(s["small_loaded"], 96)
                for i, (what, n) in enumerate(ORDER):
                    if i >= 4:
                        before, m = ORDER[i - 4]
                        for name, value in READ[before](m):
                            pe.wait_ge(s[name], value)
                    jobs[what](n, psum[:, i % 4, :])
                for before, m in ORDER[-4:]:
                    for name, value in READ[before](m):
                        pe.wait_ge(s[name], value)
                pe.wait_ge(s["qk_ready"], 5)
                pe.wait_ge(s["ck_ready"], 1)
                att_scores(0)
                for n in range(ATT_UNITS):
                    if n + 1 < ATT_UNITS:
                        att_scores(n + 1)
                    att_transpose(n)
                    if n:
                        att_values(n - 1)
                att_values(ATT_UNITS - 1)
                pe.wait_ge(s["attn_ready"], 4)
                pe.wait_ge(s["sp_ready"], 2)
                pe.wait_ge(s["cv_ready"], 2)
                pe.wait_ge(s["exp_ready"], ATT_UNITS)
                for j in range(KC):
                    if j >= 4:
                        pe.wait_ge(s["x_ready"], j - 3)
                    project(half_of(blk("wout", j // 2), j % 2), psum[:, j % 4, :], mix, "wout_mm")
                pe.wait_ge(s["x_ready"], 5)
                rms(1, psum[:, 0, :])
                for j in range(KC):
                    if j < 3:
                        pe.wait_ge(s["x_ready"], 6 + j)
                    elif j == 3:
                        pe.wait_ge(s["stat_read"], 2)
                    else:
                        pe.wait_ge(s["pq_ready"], j - 3)
                    project(half_of(blk("wq", j // 2), j % 2), psum[:, (j + 1) % 4, :], hT, "wq_mm", "h_ready", KC)
                pe.wait_ge(s["pq_ready"], KC)
                for t in range(TILES):
                    if t >= 4:
                        pe.wait_ge(s["tok_ready"], t - 3)
                    for k in range(KC):
                        m = pe.transpose(psum[:, t % 4, k * P:(k + 1) * P], hT[:, k, t * P:(t + 1) * P], ident[:])
                    m.then_inc(s["tok_mm"], 1)
                pe.wait_ge(s["tok_ready"], TILES)
                keys = blk("keys", 0)[:, 0:PEER_HEADS * N_KEYS].rearrange("p (h n) -> p h n", h=PEER_HEADS)
                for i in range(2 * TILES):
                    t, g4 = i // 2, i % 2
                    if i >= 4:
                        pe.wait_ge(s[f"key{g4}_read"], (i - 4) // 2 + 1)
                    for h in range(4):
                        for half in range(2):
                            rows = slice(64 * half, 64 * half + 64)
                            m = pe.matmul(psum[:, i % 4, half * 512 + h * P:half * 512 + (h + 1) * P],
                                          mix[rows, 4 * g4 + h, t * P:(t + 1) * P], keys[rows, 4 * g4 + h, :],
                                          start=True, stop=True)
                    m.then_inc(s["key_mm"], 1)
                pe.wait_ge(s["key0_read"], TILES)
                pe.wait_ge(s["key1_read"], TILES)
                with pe.Fori(0, TILES) as t:
                    for b in range(2):
                        pe.matmul(psum[:, 0, b * 512:(b + 1) * 512], zeros[:], cos_sin[:, 0, :], start=True, stop=False)
                    with pe.Fori(0, PEER_HEADS) as h:
                        u = t * PEER_HEADS + h
                        for k in range(TOPK):
                            pe.wait_ge(v_landed[k % V_SLOTS], 32 * (UNITS * l + u) + 16 * (k // V_SLOTS + 1))
                            pe.wait_ge(s["diag_ready"], 16 * u + k + 1)
                            for b in range(2):
                                m = pe.matmul(psum[:, 0, b * 512:(b + 1) * 512], diag[:, k % 4, :],
                                              vslot(k)[:, b * 512:(b + 1) * 512], start=False, stop=False)
                            m.then_inc(s["v_free"], 1)
                    for b in range(2):
                        m = pe.matmul(psum[:, 0, b * 512:(b + 1) * 512], zeros[:], cos_sin[:, 0, :], start=False, stop=True)
                    m.then_inc(s["acc_mm"], 1)
                    pe.wait_ge(s["acc_read"], t + 1)
                    for k in range(KC):
                        m = pe.transpose(psum[:, 1, k * P:(k + 1) * P], out_tok[:, k * P:(k + 1) * P], ident[:])
                    m.then_inc(s["back_mm"], 1)
                pe.wait_ge(s["x_added"], KC * TILES)
                pe.sem_inc(layer_done, 1)
                pe.wait_ge(layer_go, l + 1)
            for t in range(TILES):
                if t >= 4:
                    pe.wait_ge(y_copied, t - 3)
                for k in range(KC):
                    m = pe.transpose(psum[:, t % 4, k * P:(k + 1) * P], xT[:, k, t * P:(t + 1) * P], ident[:])
                m.then_inc(y_mm, 1)

        @block.scalar
        def _(act):
            n_link = [0]

            def link(ins):
                n_link[0] += 1
                ins.then_inc(s["act_link"], 1)
                act.wait_ge(s["act_link"], n_link[0])

            def squares(i):
                for k in range(KC):
                    if i:
                        act.wait_ge(s["x_ready"], k + 1)
                    if i or k >= 2:
                        act.wait_ge(s["sq_used"], KC * i + k - 1)
                    act.activation(sq[:, k % 2, :], xT[:, k, :], ACT.Square).then_inc(s["sq_ready"], 1)

            def inv_root(i, g):
                act.wait_ge(s["sq_used"], KC * (i + 1))
                act.activation(rstd[:], g[:, 0:TOK], ACT.Ln, bias=eps).then_inc(s["stat_read"], 1)
                act.wait_ge(s["stat_read"], i + 1)
                act.activation(rstd[:], rstd[:], ACT.Exp, scale=-0.5).then_inc(s["rstd_ready"], 1)

            def modulate(i, k):
                shift, scale = ((SH_M, SC_M), (SH_F, SC_F))[i]
                act.wait_ge(s["scale_ready"], i + 1)
                act.wait_ge(s["xn_ready"], KC * i + k + 1)
                for st, cols in enumerate((slice(0, LAT), slice(LAT, TOK))):
                    m = act.activation(hT[:, k, cols], hT[:, k, cols], ACT.Identity,
                                       bias=modT[:, shift + k, st:st + 1], scale=modT[:, scale + k, st:st + 1])
                m.then_inc(s["h_ready"], 1)

            def rms(n, g):
                inv_root(0, g)

            def mod(n, g):
                act.wait_ge(s["mod_mm"], n + 1)
                if n >= 2:
                    act.wait_ge(s["modT_mm"], n - 1)
                act.copy(mod_row[0:2, n % 2, :], g[0:2, 0:512]).then_inc(s["modrow_ready"], 1)
                if n >= 8:
                    modulate(0, 2 * (n - 8))
                    modulate(0, 2 * (n - 8) + 1)

            def sine(i):
                act.wait_ge(s["arg_ready"], i + 1)
                act.activation(sin_out[0:HY_FFN, i, :], sin_arg[0:HY_FFN, 0, :], ACT.Sin).then_inc(s["sin_ready"], 1)

            def f3(t, g):
                if t == 0:
                    link(act.activation(decay, decay, ACT.Abs))
                if t >= 2:
                    act.wait_ge(s["ab_ready"], t - 1)
                act.activation(envelope[:, t % 2, :], decay, ACT.Exp, scale=neg_time[:, t:t + 1]).then_inc(s["env_ready"], 1)

            def hf(c, g):
                act.wait_ge(s["hf_mm"], c + 1)
                act.copy(filt[:, c, :, :].rearrange("p r n -> p (r n)"), g[:, 0:512]).then_inc(s["filt_ready"], 1)

            def qk(n, g):
                act.wait_ge(s["qk_mm"], n + 1)
                if n >= 2:
                    act.wait_ge(s["hs_mm"], n - 1)
                act.activation(sq[:, n % 2, :], g[:, 0:TOK], ACT.Square).then_inc(s["hsq_ready"], 1)

            def hs(n, g):
                act.wait_ge(s["hs_mm"], n + 1)
                if n >= 2:
                    act.wait_ge(s["qn_ready"], n - 1)
                act.activation(tmp[:, n % 2, 0:TOK], g[:, 0:TOK], ACT.Ln, bias=eps).then_inc(s["hs_read"], 1)
                act.wait_ge(s["hs_read"], n + 1)
                act.activation(tmp[:, n % 2, 0:TOK], tmp[:, n % 2, 0:TOK], ACT.Exp, scale=-0.5).then_inc(s["hr_ready"], 1)

            def vt(t, g):
                act.wait_ge(s["vt_mm"], t + 1)
                act.copy(v_tok[:, t, :], g[:, 0:P])
                act.activation(sg_v[:, t, :], g[:, P:P + SG_W], ACT.Gelu_apprx_tanh).then_inc(s["vt_read"], 1)
                if t == TILES - 1:
                    act.wait_ge(s["vt_read"], TILES)
                    for i in range(TILES):
                        link(act.activation(sg_junk, sg_v[:, i, :], ACT.Square, accum_out=ssq[:, i:i + 1]))
                    link(act.activation(sg_rstd, ssq, ACT.Ln, bias=eps, scale=1.0 / SG_W))
                    act.activation(sg_rstd, sg_rstd, ACT.Exp, scale=-0.5).then_inc(s["sgr_ready"], 1)

            def ko(n, g):
                act.wait_ge(s["ko_mm"], 1)
                act.copy(k_out, g[:, 0:P]).then_inc(s["ko_ready"], 1)

            def hy(i, g):
                act.wait_ge(s["hy_mm"], i + 1)
                if i == 0:
                    act.wait_ge(s["pads_ready"], 1)
                if i >= 2:
                    act.wait_ge(s["hy_conv"], i - 1)
                if i == 2:
                    act.wait_ge(s["gu_ready"], 1)
                cc = HY_CHUNK[i]
                for a, b, w in PIECES:
                    act.copy(raw[:, i % 2, b + 1:b + 1 + w], g[:, a:a + w])
                for a, b, w in PIECES:
                    m = act.activation(hy_dst(i)[:, b:b + w], g[:, a:a + w], ACT.Identity,
                                       bias=par[:, S_CONVB + cc:S_CONVB + cc + 1],
                                       scale=par[:, S_CONVW + 6 + cc:S_CONVW + 6 + cc + 1])
                m.then_inc(s["hy_read"], 1)

            def su(j, g):
                act.wait_ge(s["su_mm"], j + 1)
                act.activation(mix[:, 6 + j, :], g[:, 0:TOK], ACT.Gelu_apprx_tanh).then_inc(s["su_ready"], 1)

            def ut(n, g):
                act.wait_ge(s["ut_mm"], n + 1)
                dst = (uT[:, 0:LAT_TILES, :] if n == 0 else uT[:, LAT_TILES:, :]).rearrange("p t n -> p (t n)")
                act.copy(dst, g[:, 0:(1024 if n == 0 else 256)]).then_inc(s["ut_ready"], 1)

            jobs = {"rms": rms, "mod": mod, "f1": lambda n, g: sine(0), "f2": lambda n, g: sine(1), "f3": f3, "hf": hf,
                    "qk": qk, "hs": hs, "vt": vt, "ko": ko, "hy": hy, "su": su, "ut": ut}

            def att_exp(n):
                width = unit_of(n)[3]
                act.wait_ge(s["max_ready"], n + 1)
                if n >= 2:
                    act.wait_ge(s["pt_mm"], n - 1)
                act.activation(probs[:, n % 2, 0:width], psum[:, n % 2, 0:width], ACT.Exp, bias=negmax[:, n % 2:n % 2 + 1],
                               accum_out=rowsum[:, n % 2:n % 2 + 1]).then_inc(s["exp_ready"], 1)

            def att_copy(n):
                width = unit_of(n)[3]
                act.wait_ge(s["pt_mm"], n + 1)
                if n >= 2:
                    act.wait_ge(s["pv_mm"], n - 1)
                act.copy(probsT[:, n % 2, 0:width], psum[:, 2, 0:width]).then_inc(s["pt_ready"], 1)

            act.wait_ge(const_loaded, 144)
            act.activation(csil, csil, ACT.Silu).then_inc(silu_ready, 1)
            with act.Fori(0, DEPTH) as l:
                n_link[0] = 0
                act.wait_ge(s["small_loaded"], 96)
                squares(0)
                for i, (what, n) in enumerate(ORDER):
                    if what in jobs:
                        jobs[what](n, psum[:, i % 4, :])
                att_exp(0)
                for n in range(ATT_UNITS):
                    if n + 1 < ATT_UNITS:
                        att_exp(n + 1)
                    att_copy(n)
                squares(1)
                inv_root(1, psum[:, 0, :])
                for k in range(KC):
                    modulate(1, k)
                for j in range(KC):
                    act.wait_ge(s["wq_mm"], j + 1)
                    act.copy(mix[:, j, :], psum[:, (j + 1) % 4, 0:TOK]).then_inc(s["pq_ready"], 1)
                for t in range(TILES):
                    act.wait_ge(s["key_mm"], 2 * t + 1)
                    act.copy(scores[:, t * 8:t * 8 + 4, :, :].rearrange("p u h n -> p h u n"),
                             psum[:, 2 * t % 4, :].rearrange("p (h u n) -> p h u n", h=2, u=4)).then_inc(s["key0_read"], 1)
                act.wait_ge(s["key0_read"], TILES)
                act.wait_ge(s["key1_read"], TILES)
                act.copy(unit_s, scores[:, 0, :, :]).then_inc(s["staged"], 1)
                act.wait_ge(s["best_ready"], 1)
                act.activation(gate_e[:], best[:], ACT.Exp, bias=gate_s[:, 1:2], accum_out=gate_s[:, 0:1]).then_inc(s["gexp_ready"], 1)
                with act.Fori(0, TILES) as t:
                    with act.Fori(0, PEER_HEADS) as h:
                        u = t * PEER_HEADS + h
                        act.wait_ge(s["idx_ready"], u + 1)
                        act.copy(unit_s.rearrange("p h n -> p (h n)"),
                                 scores.rearrange("p u h n -> p (u h n)")[:, bass.ds((u + 1) * 256, 256)]).then_inc(s["staged"], 1)
                        act.wait_ge(s["u_free"], U_SLOTS + 16 * u + 16)
                        act.activation(acts[:], dots[:], ACT.Gelu_apprx_tanh).then_inc(s["gelu_ready"], 1)
                        act.wait_ge(s["w_ready"], u + 1)
                        for k in range(TOPK):
                            act.wait_ge(s["v_free"], V_SLOTS + 16 * u + k - 3)
                            act.activation(diag[:, k % 4, :], ident[:], ACT.Copy, scale=wts[:, k:k + 1]).then_inc(s["diag_ready"], 1)
                        act.wait_ge(s["best_ready"], u + 2)
                        act.activation(gate_e[:], best[:], ACT.Exp, bias=gate_s[:, 1:2], accum_out=gate_s[:, 0:1]
                                       ).then_inc(s["gexp_ready"], 1)
                    act.wait_ge(s["acc_mm"], t + 1)
                    act.copy(out_tok, psum[:, 0, :]).then_inc(s["acc_read"], 1)
                act.sem_inc(layer_done, 1)
                act.wait_ge(layer_go, l + 1)
            for t in range(TILES):
                act.wait_ge(y_mm, t + 1)
                if t >= 2:
                    act.wait_ge(y_stored[t % 2], 16 * (t // 2))
                act.copy(tmp[:, t % 2, :], psum[:, t % 4, :]).then_inc(y_copied, 1)

        @block.vector
        def _(dve):
            n_link = [0]

            def link(ins):
                n_link[0] += 1
                ins.then_inc(s["dve_link"], 1)
                dve.wait_ge(s["dve_link"], n_link[0])

            def normalise(i):
                dve.wait_ge(s["rstd_ready"], i + 1)
                for k in range(KC):
                    dve.tensor_tensor(hT[:, k, :], xT[:, k, :], rstd[:], ALU.mult).then_inc(s["xn_ready"], 1)

            def rms(n, g):
                normalise(0)

            def mod_scale(sc, gain):
                for st in range(2):
                    m = dve.scalar_tensor_tensor(out=modT[:, sc:sc + KC, st], in0=modT[:, sc:sc + KC, st], scalar=1.0,
                                                 in1=par[:, gain:gain + KC], op0=ALU.add, op1=ALU.mult)
                    if st == 0:
                        link(m)
                m.then_inc(s["scale_ready"], 1)

            def modT_(n, g):
                dve.wait_ge(s["modT_mm"], n + 1)
                dve.tensor_tensor(modT[:, 4 * n:4 * n + 4, :], g[:, 0:8].rearrange("p (j s) -> p j s", s=2),
                                  par[:, S_ADAB + 4 * n:S_ADAB + 4 * n + 4].unsqueeze(2).broadcast_to([P, 4, 2]),
                                  ALU.add).then_inc(s["mod_ready"], 1)
                dve.wait_ge(s["mod_ready"], n + 1)
                if n == 3:
                    mod_scale(SC_M, S_GMIX)
                if n == 9:
                    mod_scale(SC_F, S_GFFN)
                if n == 11:
                    for t in range(TILES):
                        st = 0 if t < LAT_TILES else 1
                        link(dve.tensor_copy(gate_f[:, t * KC:(t + 1) * KC], modT[:, G_F:G_F + KC, st]))

            def sine_arg(i, g):
                dve.wait_ge(s["filt_mm"], i + 1)
                a, r = sin_arg[0:HY_FFN, 0, :], sin_arg[0:HY_FFN, 1, :]
                fb, fr = ((S_FB1, S_FR1), (S_FB2, S_FR2))[i]
                if i:
                    dve.wait_ge(s["sin_ready"], 1)
                link(dve.tensor_scalar(a, g[0:HY_FFN, 0:TOK], par[0:HY_FFN, fb:fb + 1], par[0:HY_FFN, fr:fr + 1], ALU.add, ALU.mult))
                link(dve.tensor_scalar(r, a, 1.0 / TWO_PI, ROUND, ALU.mult, ALU.add))
                link(dve.tensor_scalar(r, r, -ROUND, None, ALU.add))
                for c in (PI_HI, PI_MID, PI_LO):
                    link(dve.scalar_tensor_tensor(out=a, in0=r, scalar=-c, in1=a, op0=ALU.mult, op1=ALU.add))
                dve.tensor_scalar(a, a, SIN_MAX, -SIN_MAX, ALU.min, ALU.max).then_inc(s["arg_ready"], 1)

            def f3(t, g):
                dve.wait_ge(s["filt_mm"], t + 3)
                dve.wait_ge(s["env_ready"], t + 1)
                if t in (0, LAT_TILES):
                    link(dve.memset(envelope[0:1, t % 2, HY_CH:], 0.0))
                if t:
                    dve.wait_ge(s["ab_ready"], t)
                h = x1[:, 0:512]
                link(dve.tensor_tensor(h, g[:, 0:512], envelope[:, t % 2, :], ALU.mult))
                dve.tensor_tensor(filt_ab[:, t, 0, :], h[:, 0:HY_CH], h[:, HY_CH:], ALU.add)
                dve.tensor_tensor(filt_ab[:, t, 1, :], h[:, 0:HY_CH], h[:, HY_CH:], ALU.subtract).then_inc(s["ab_ready"], 1)

            def qk(n, g):
                dve.wait_ge(s["hsq_ready"], n + 1)
                col = S_KG if n == 0 else S_QG
                dve.tensor_scalar(qk_dst(n), g[:, 0:TOK], par[:, col:col + 1], 1.0 if n == 0 else HEAD_DIM ** -0.5,
                                  ALU.mult, ALU.mult).then_inc(s["qg_ready"], 1)

            def hs(n, g):
                dve.wait_ge(s["hr_ready"], n + 1)
                dve.wait_ge(s["qg_ready"], n + 1)
                dve.tensor_tensor(qk_dst(n), qk_dst(n), tmp[:, n % 2, 0:TOK], ALU.mult).then_inc(s["qn_ready"], 1)

            def rot(n, g):
                dve.wait_ge(s["rot_mm"], n + 1)
                x = qk_dst(n)[:, 0:LAT]
                if n:
                    dve.wait_ge(s["qk_ready"], n)
                if n == 4:
                    dve.wait_ge(s["y_ready"], 1)
                link(dve.tensor_tensor(work, g[:, 0:LAT], cos_sin[:, 1, :], ALU.mult))
                link(dve.tensor_tensor(x, x, cos_sin[:, 0, :], ALU.mult))
                dve.tensor_tensor(x, x, work, ALU.add).then_inc(s["qk_ready"], 1)

            def vt(t, g):
                if t == TILES - 1:
                    dve.wait_ge(s["sgr_ready"], 1)
                    for i in range(TILES):
                        dve.scalar_tensor_tensor(out=sg_v[:, i, :], in0=sg_v[:, i, :], scalar=sg_rstd[:, i:i + 1],
                                                 in1=sg_gain, op0=ALU.mult, op1=ALU.mult).then_inc(s["sgn_ready"], 1)

            def ck(n, g):
                dve.wait_ge(s["ck_mm"], 1)
                dve.tensor_copy(kT[:, 0:PAST], g[:, 0:P]).then_inc(s["ck_ready"], 1)

            def hy(i, g):
                if i == 0:
                    dve.wait_ge(s["hf_mm"], 5)
                    for b in range(2):
                        for a, w in ((0, 1), (LAT + 1, 2), (PAD - 1, 1)):
                            dve.memset(raw[:, b, a:a + w], 0.0)
                        dve.memset(x0[:, b, LAT:LAT + 2], 0.0)
                        dve.memset(gate_u[:, b, LAT:LAT + 2], 0.0)
                    dve.memset(x1[:, LAT:LAT + 2], 0.0).then_inc(s["pads_ready"], 1)
                dve.wait_ge(s["hy_read"], i + 1)
                cc, dst = HY_CHUNK[i], hy_dst(i)
                for tap, step in ((0, link), (2, lambda ins: ins.then_inc(s["hy_conv"], 1))):
                    step(dve.scalar_tensor_tensor(out=dst[:, 0:CONV], in0=raw[:, i % 2, tap:tap + CONV],
                                                  scalar=par[:, S_CONVW + 6 * tap + cc:S_CONVW + 6 * tap + cc + 1],
                                                  in1=dst[:, 0:CONV], op0=ALU.mult, op1=ALU.add))
                if i in (1, 3):
                    dve.wait_ge(s["hy_conv"], i + 1)
                    dve.tensor_tensor(dst[:, 0:CONV], dst[:, 0:CONV], x1[:, 0:CONV], ALU.mult).then_inc(s["gu_ready"], 1)

            def sp_(j, g):
                dve.wait_ge(s["sp_mm"], j + 1)
                dve.wait_ge(s["su_ready"], 2)
                dve.wait_ge(s["gu_ready"], 2)
                if j:
                    dve.wait_ge(s["sp_ready"], j)
                link(dve.tensor_tensor(x1[:, 0:TOK].rearrange("p (t n) -> p t n", t=TILES),
                                       g[:, 0:TOK].rearrange("p (t n) -> p t n", t=TILES),
                                       sg_bias[:, j, :].unsqueeze(1).broadcast_to([P, TILES, P]), ALU.add))
                dve.tensor_tensor(mix[:, 6 + j, :], mix[:, 6 + j, :], x1[:, 0:TOK], ALU.mult).then_inc(s["sp_ready"], 1)

            def df(c, g):
                dve.wait_ge(s["df_mm"], c + 1)
                dve.wait_ge(s["filt_ready"], c + 1)
                dve.wait_ge(s["sp_ready"], 2)
                if c:
                    dve.wait_ge(s["y_ready"], c)
                H = filt[:, c, :, :].rearrange("p r n -> p (r n)")
                link(dve.tensor_tensor(x1[:, 0:512], g[:, 0:512], H, ALU.mult))
                dve.wait_ge(s["qk_ready"], 4 if c == 0 else 5)
                link(dve.tensor_tensor(work[:, 0:HY_CH], g[:, 0:HY_CH], H[:, HY_CH:], ALU.mult))
                link(dve.tensor_tensor(work[:, HY_CH:], g[:, HY_CH:512], H[:, 0:HY_CH], ALU.mult))
                link(dve.tensor_tensor(H[:, 0:HY_CH], x1[:, 0:HY_CH], x1[:, HY_CH:512], ALU.subtract))
                dve.tensor_tensor(H[:, HY_CH:], work[:, 0:HY_CH], work[:, HY_CH:], ALU.add).then_inc(s["y_ready"], 1)

            def cv(j, g):
                dve.wait_ge(s["cv_mm"], j + 1)
                if j:
                    dve.wait_ge(s["cv_ready"], j)
                for a, b, w in PIECES:
                    link(dve.scalar_tensor_tensor(out=x1[:, b:b + w], in0=gate_u[:, j, b:b + w],
                                                  scalar=par[:, S_SKIP + j:S_SKIP + j + 1], in1=g[:, a:a + w],
                                                  op0=ALU.mult, op1=ALU.add))
                for i, (a, b, w) in enumerate(PIECES):
                    m = dve.tensor_tensor(mix[:, 4 + j, a:a + w], x1[:, b:b + w], x0[:, j, b:b + w], ALU.mult)
                m.then_inc(s["cv_ready"], 1)

            jobs = {"rms": rms, "modT": modT_, "f1": lambda n, g: sine_arg(0, g), "f2": lambda n, g: sine_arg(1, g),
                    "f3": f3, "qk": qk, "hs": hs, "rot": rot, "vt": vt, "ck": ck, "hy": hy, "sp": sp_, "df": df, "cv": cv}

            def att_max(n):
                width = unit_of(n)[3]
                dve.wait_ge(s["sc_mm"], n + 1)
                dve.tensor_reduce(negmax[:, n % 2:n % 2 + 1], psum[:, n % 2, 0:width], AX.X, ALU.max, negate=True
                                  ).then_inc(s["max_ready"], 1)

            def att_norm(n):
                width = unit_of(n)[3]
                dve.wait_ge(s["exp_ready"], n + 1)
                link(dve.reciprocal(rinv[:, n % 2:n % 2 + 1], rowsum[:, n % 2:n % 2 + 1]))
                dve.tensor_scalar(probs[:, n % 2, 0:width], probs[:, n % 2, 0:width], rinv[:, n % 2:n % 2 + 1], None,
                                  ALU.mult).then_inc(s["probs_ready"], 1)

            def top16(vals, idxs, src, step):
                step(dve.max(vals[:, 0:8], src))
                step(dve.max_index(idxs[:, 0:8], vals[:, 0:8], src))
                step(dve.match_replace(src, vals[:, 0:8], src, -3.0e38))
                step(dve.max(vals[:, 8:16], src))
                step(dve.max_index(idxs[:, 8:16], vals[:, 8:16], src))

            def pick(v):
                count = [0]

                def step(ins):
                    count[0] += 1
                    ins.then_inc(s["topk_link"], 1)
                    dve.wait_ge(s["topk_link"], TOPK_LINKS * v + count[0])
                    if count[0] not in STEPS_BEFORE_PLAIN:
                        dve.sem_inc(dve_tick, 1)

                dve.wait_ge(s["staged"], v + 1)
                dve.sem_inc(dve_tick, 1)
                for half in range(2):
                    top16(topv[:, half, :], topi[:, half, :], unit_s[:, half, :], step)
                grid = [P, TOPK, TOPK]
                step(dve.tensor_tensor(cand.rearrange("p (a b) -> p a b", a=TOPK), topv[:, 0, :].unsqueeze(2).broadcast_to(grid),
                                       topv[:, 1, :].unsqueeze(1).broadcast_to(grid), ALU.add))
                top16(best[:], pos[:], cand, step)
                dve.tensor_scalar(gate_s[:, 1:2], best[:, 0:1], -1.0, None, ALU.mult).then_inc(s["best_ready"], 1)
                step(dve.tensor_scalar(posij[:, 0, :], pos[:], 4, None, ALU.logical_shift_right))
                step(dve.tensor_scalar(posij[:, 1, :], pos[:], TOPK - 1, None, ALU.bitwise_and))
                step(dve.tensor_copy(posf, posij))
                step(dve.tensor_copy(topf, topi))
                for half in range(2):
                    oh = onehot.rearrange("p (a b) -> p a b", a=TOPK)
                    step(dve.tensor_tensor(oh, iota16.unsqueeze(1).broadcast_to(grid),
                                           posf[:, half, :].unsqueeze(2).broadcast_to(grid), ALU.is_equal))
                    step(dve.tensor_tensor(oh, oh, topf[:, half, :].unsqueeze(1).broadcast_to(grid), ALU.mult))
                    step(dve.tensor_reduce(picked[:, half, :], oh, AX.X, ALU.add))
                step(dve.scalar_tensor_tensor(out=idxf[:], in0=picked[:, 0, :], scalar=float(N_KEYS), in1=picked[:, 1, :],
                                              op0=ALU.mult, op1=ALU.add))
                assert count[0] == TOPK_LINKS, count
                dve.tensor_scalar(idx_all[:, bass.ds(v * TOPK, TOPK)], idxf[:], layer_base, None, ALU.add
                                  ).then_inc(s["idx_ready"], 1)

            dve.memset(layer_base, 0.0)
            dve.memset(zeros[:], 0.0).then_inc(zero_ready, 1)
            dve.wait_ge(zero_ready, 1)
            dve.wait_ge(const_loaded, 144)
            with dve.Fori(0, DEPTH) as l:
                n_link[0] = 0
                dve.wait_ge(s["small_loaded"], 96)
                for i, (what, n) in enumerate(ORDER):
                    if what in jobs:
                        jobs[what](n, psum[:, i % 4, :])
                att_max(0)
                for n in range(ATT_UNITS):
                    if n + 1 < ATT_UNITS:
                        att_max(n + 1)
                    att_norm(n)
                    if n % 10 == 0 and n or n == ATT_UNITS - 1:
                        c = (n - 1) // 10
                        dve.wait_ge(s["pv_mm"], 10 * (c + 1))
                        dve.tensor_copy(mix[:, c, :], psum[:, 3, 0:TOK]).then_inc(s["attn_ready"], 1)
                for j in range(KC):
                    dve.wait_ge(s["wout_mm"], j + 1)
                    for st, cols in enumerate((slice(0, LAT), slice(LAT, TOK))):
                        m = dve.scalar_tensor_tensor(out=xT[:, j, cols], in0=psum[:, j % 4, cols],
                                                     scalar=modT[:, G_M + j, st:st + 1], in1=xT[:, j, cols],
                                                     op0=ALU.mult, op1=ALU.add)
                    m.then_inc(s["x_ready"], 1)
                normalise(1)
                for t in range(TILES):
                    dve.wait_ge(s["tok_mm"], t + 1)
                    dve.tensor_copy(h_tok[:, t * D_MODEL:(t + 1) * D_MODEL], psum[:, t % 4, :]).then_inc(s["tok_ready"], 1)
                for t in range(TILES):
                    dve.wait_ge(s["key_mm"], 2 * t + 2)
                    if t == 0:
                        link(dve.memset(scores[:, UNITS, :, :], 0.0))
                    dve.tensor_copy(scores[:, t * 8 + 4:t * 8 + 8, :, :].rearrange("p u h n -> p h u n"),
                                    psum[:, (2 * t + 1) % 4, :].rearrange("p (h u n) -> p h u n", h=2, u=4)
                                    ).then_inc(s["key1_read"], 1)
                pick(0)
                with dve.Fori(0, TILES) as t:
                    with dve.Fori(0, PEER_HEADS) as h:
                        u = t * PEER_HEADS + h
                        for k in range(TOPK):
                            dve.wait_ge(u_landed[k % U_SLOTS], 32 * (UNITS * l + u) + 16 * (k // U_SLOTS + 1))
                            dve.scalar_tensor_tensor(out=uslot(k), in0=uslot(k), scalar=1.0,
                                                     in1=h_tok[:, bass.ds(t * D_MODEL, D_MODEL)], op0=ALU.mult, op1=ALU.mult,
                                                     accum_out=dots[:, k:k + 1]).then_inc(s["u_free"], 1)
                        dve.wait_ge(s["gexp_ready"], u + 1)
                        dve.reciprocal(gate_s[:, 2:3], gate_s[:, 0:1]).then_inc(s["wlink"], 1)
                        dve.wait_ge(s["wlink"], u + 1)
                        dve.wait_ge(s["gelu_ready"], u + 1)
                        dve.scalar_tensor_tensor(out=wts[:], in0=acts[:], scalar=gate_s[:, 2:3], in1=gate_e[:],
                                                 op0=ALU.mult, op1=ALU.mult).then_inc(s["w_ready"], 1)
                        dve.wait_ge(s["w_ready"], u + 1)
                        pick(u + 1)
                    dve.wait_ge(s["back_mm"], t + 1)
                    for k in range(KC):
                        x = xT[:, k, bass.ds(t * P, P)]
                        dve.scalar_tensor_tensor(out=x, in0=psum[:, 1, k * P:(k + 1) * P], scalar=gate_f[:, bass.ds(t * KC + k, 1)],
                                                 in1=x, op0=ALU.mult, op1=ALU.add).then_inc(s["x_added"], 1)
                link(dve.tensor_scalar(layer_base, layer_base, float(N_EXPERTS), None, ALU.add))
                dve.sem_inc(layer_done, 1)
                dve.wait_ge(layer_go, l + 1)


def _columns():
    def run(a, n=P):
        return list(range(a, a + n))

    hy0, sg0 = 768, 1536
    x0, x1, v = hy0, hy0 + HY_CH, hy0 + 2 * HY_CH
    q = [run(c * 64, 64) + run((c + 4) * 64, 64) for c in range(4)]
    return [run(512), run(640), run(sg0 + 256), run(sg0 + 384), run(x1), run(v), run(x1 + P), run(v + P),
            run(x0), run(x0 + P), run(sg0), run(sg0 + P), *q]


def _blocks(w, cols):
    l, r, _ = w.shape
    w = w[:, :, np.concatenate([np.asarray(c) for c in cols])].reshape(l, r // P, P, len(cols) // 2, 2, P)
    return np.ascontiguousarray(w.transpose(0, 3, 2, 4, 1, 5)).reshape(l, len(cols) // 2, P, BLOCK)


def _constants():
    f = np.float32
    c = np.zeros((5, P, P), f)
    c[0] = np.eye(P, dtype=f)
    c[1] = 1.0 / D_MODEL
    c[2] = np.kron(np.eye(2), np.full((64, 64), 1.0 / HEAD_DIM)).astype(f)
    i = np.arange(0, P, 2)
    c[3][i + 1, i], c[3][i, i + 1] = -1.0, 1.0
    time = [np.arange(n, dtype=f) / f(n - 1) for n in (LAT, CTX)]
    c[4][:, 0:TILES] = -np.concatenate(time).reshape(TILES, P).T
    c[4][:, TILES] = EPS
    c[4][:, TILES + 1:TILES + 1 + TOPK] = np.arange(TOPK)
    inv = f(ROPE_THETA) ** (-np.arange(HEAD_DIM // 4, dtype=f) / f(HEAD_DIM // 4))
    t = np.arange(LAT)
    ang = np.concatenate([(t // GRID_W).astype(f)[:, None] * inv, (t % GRID_W).astype(f)[:, None] * inv], -1)
    ang = ang[:, np.arange(P) % HEAD_DIM // 2].T
    rope = np.stack([np.cos(ang), np.sin(ang)], 1).astype(f)

    def waves(n):
        a = np.pi * (2 * np.arange(n)[None, :] + 1) * np.arange(n)[:, None] / (2 * n)
        return np.cos(a), np.sin(a)

    feats = []
    for n, tn in zip((LAT, CTX), time):
        w = f(2.0 * np.pi) * np.arange(n, dtype=f) / f(n)
        z = w[:, None] * np.linspace(1e-4, HY_BANDS - 1, HY_BANDS, dtype=f)[None, :]
        feats.append(np.concatenate([tn[:, None], np.cos(z), -np.sin(z)], -1))
    feats = np.ascontiguousarray(np.concatenate(feats).T.astype(f))
    co, si = waves(LAT)
    dft = np.stack([m.reshape(LAT // P, P, LAT).transpose(1, 0, 2).reshape(P, BLOCK)
                    for m in (co, si, co.T / LAT, si.T / LAT)]).astype(f)
    co, si = waves(CTX)
    dft_ctx = np.stack([co, si, co.T / CTX, si.T / CTX], 1).astype(f)
    return c, rope, feats, dft, dft_ctx


def kernel(**inputs):
    import concourse.bacc as _bacc
    from concourse.bass_utils import run_bass_kernel_spmd as _run

    x = {k: np.asarray(v) for k, v in inputs.items()}
    f = np.float32
    L = DEPTH
    consts, rope, feats, dft, dft_ctx = _constants()

    def byP(a):
        return a.reshape(L, -1, P).transpose(0, 2, 1)

    small = np.zeros((L, P, S_COLS), f)
    small[:, :, S_GMIX:S_GMIX + KC] = byP(x["norm_mix_g"])
    small[:, :, S_GFFN:S_GFFN + KC] = byP(x["norm_ffn_g"])
    small[:, :, S_ADAB:S_ADAB + 6 * KC] = byP(x["ada_b"])
    small[:, :, S_QG] = np.concatenate([x["q_norm_g"]] * 2, 1)
    small[:, :, S_KG] = np.concatenate([x["k_norm_g"]] * 2, 1)
    for tap in range(3):
        small[:, :, S_CONVW + 6 * tap:S_CONVW + 6 * tap + 6] = byP(x["hy_conv_w"][:, tap])
    small[:, :, S_CONVB:S_CONVB + 6] = byP(x["hy_conv_b"])
    for col, name in ((S_FR1, "hy_freq1"), (S_FB1, "hy_fb1"), (S_FR2, "hy_freq2"), (S_FB2, "hy_fb2")):
        small[:, 0:HY_FFN, col] = x[name]
    small[:, :, S_SKIP:S_SKIP + 2] = byP(x["hy_skip"])
    wide = np.zeros((L, P, SG_W + 2 * P), f)
    wide[:, :, 0:SG_W] = x["sg_norm_g"][:, None, :]
    wide[:, :, SG_W:] = np.repeat(x["sg_b"].reshape(L, 2, 2, P), 64, axis=2).transpose(0, 2, 1, 3).reshape(L, P, 2 * P)
    fw12 = np.zeros((L, HY_FFN, 2 * HY_FFN + 512), f)
    fw12[:, 0:HY_EMB, 0:HY_FFN] = x["hy_fw1"]
    fw12[:, :, HY_FFN:2 * HY_FFN] = x["hy_fw2"]
    fw12[:, :, 2 * HY_FFN:] = x["hy_fw3"]
    blocks128 = [range(a, a + P) for a in range(0, D_MODEL, P)]
    heads = np.concatenate([np.r_[c * 64:c * 64 + 64, (c + 4) * 64:(c + 4) * 64 + 64] for c in range(4)])
    rows = np.concatenate([heads, np.arange(512, D_MODEL)])
    ada = x["ada_w"].reshape(L, 2, 4, P, N_MOD_BLOCKS, 512).transpose(0, 4, 1, 3, 2, 5).reshape(L, 2 * N_MOD_BLOCKS, P, BLOCK)
    tokens = np.concatenate([x["x_sample"][0], x["x_prompt"][0]], 0)
    arrays = {
        "xT_in": tokens.T.reshape(KC, P, TOK).transpose(1, 0, 2),
        "cT_in": np.stack([x["c"][0], x["c_ctx"]], -1).reshape(KC, P, 2).transpose(1, 0, 2),
        "cache_k": x["cache_k"][0].reshape(L, PAST, 2 * HEAD_DIM), "cache_v": x["cache_v"][0].reshape(L, PAST, 2 * HEAD_DIM),
        "ada": ada, "win": _blocks(x["w_in"], _columns()), "wout": _blocks(x["w_out"][:, rows], blocks128),
        "wq": _blocks(x["peer_wq"], blocks128), "dft": dft, "dft_ctx": dft_ctx, "small": small, "wide": wide,
        "decays": np.broadcast_to(x["hy_decay"].reshape(L, 1, 512), (L, P, 512)), "fw12": fw12,
        "featsT": feats, "sgw": x["sg_w"].transpose(0, 3, 1, 2),
        "keysT": x["peer_keys"].transpose(0, 2, 4, 1, 3).reshape(L, P, PEER_HEADS, N_KEYS), "rope": rope, "consts": consts,
        "peer_u": x["peer_u"].reshape(L * N_EXPERTS, D_MODEL), "peer_v": x["peer_v"].reshape(L * N_EXPERTS, D_MODEL),
    }
    arrays = {f"in_{k}": np.ascontiguousarray(v) for k, v in arrays.items()}
    outs = {"y_prompt": [CTX, D_MODEL], "y_sample": [LAT, D_MODEL], "new_k": [L, CTX, P], "new_v": [L, CTX, P]}
    nc = _bacc.Bacc("TRN2", target_bir_lowering=False, num_devices=1)
    args = {k[3:]: nc.dram_tensor(k, a.shape, mybir.dt.from_np(a.dtype), kind="ExternalInput").ap() for k, a in arrays.items()}
    for k, shape in outs.items():
        args[k] = nc.dram_tensor(f"out_{k}", shape, F32, kind="ExternalOutput").ap()
    mixer_peer_kernel(nc, **args)
    r = _run(nc, [arrays], core_ids=[0]).results[0]
    cache = (1, L, CTX, 2, HEAD_DIM)
    return (r["out_y_prompt"].reshape(1, CTX, D_MODEL), r["out_y_sample"].reshape(1, LAT, D_MODEL),
            r["out_new_k"].reshape(cache), r["out_new_v"].reshape(cache))
```

```python
from contextlib import ExitStack

import numpy as np

import concourse.bass as bass
from concourse import mybir

F32 = mybir.dt.float32
U32 = mybir.dt.uint32
ALU = mybir.AluOpType
ACT = mybir.ActivationFunctionType
AX = mybir.AxisListType

P = 128
D_MODEL = 1024
DEPTH = 2
LAT = 512
CTX = 128
TOK = LAT + CTX
PAST = 128
GRID_W = 64
EPS = 1e-6
HEAD_DIM = 64
ROPE_THETA = 10000.0
HY_CH = 256
HY_BANDS = 16
HY_EMB = 1 + 2 * HY_BANDS
HY_FFN = 64
SG_W = 256
PEER_HEADS = 8
N_KEYS = 128
TOPK = 16
N_EXPERTS = N_KEYS * N_KEYS

KC = D_MODEL // P
TILES = TOK // P
LAT_TILES = LAT // P
N_MOD_BLOCKS = 6 * D_MODEL // 512
BLOCK = 2048
SLOTS = 4
ROWS = 4
IDX_PLACES = 4
SMALL_LOADS = 8
CONST_LOADS = 7

L_, C_ = 0, 1
WIDTH = (LAT, CTX)
COLS = (slice(0, LAT), slice(LAT, TOK))
NT = (LAT_TILES, 1)
TILE0 = (0, LAT_TILES)

S_GMIX = 0
S_GFFN = S_GMIX + KC
S_ADAB = S_GFFN + KC
S_QG = S_ADAB + 6 * KC
S_KG = S_QG + 1
S_CONVW = S_KG + 1
S_CONVB = S_CONVW + 18
S_FR1 = S_CONVB + 6
S_FB1 = S_FR1 + 1
S_FR2 = S_FB1 + 1
S_FB2 = S_FR2 + 1
S_SKIP = S_FB2 + 1
S_COLS = S_SKIP + 2

TWO_PI = 2.0 * np.pi
PI_HI = 6.28125
PI_MID = float(np.float32(TWO_PI - PI_HI))
PI_LO = float(np.float32(TWO_PI - PI_HI - PI_MID))
ROUND = 1.5 * 2.0 ** 23
SIN_MAX = 3.1415925

ATT_UNITS = tuple(8 * n for n in NT)


def attention_jobs(l, st):
    n_units = ATT_UNITS[st]
    jobs = [("fence", l, st, 0), ("as", l, st, 0), ("as", l, st, 1)]
    for n in range(n_units):
        jobs += [("as", l, st, n + 2)] if n + 2 < n_units else []
        jobs += [("at", l, st, n)] + ([("av", l, st, n - 1)] if n else [])
    return jobs + [("av", l, st, n_units - 1), ("fence", l, st, 1)]


def phase(l, st):
    return 2 * l + (st == L_)


def mixer_jobs(l, st):
    def js(text):
        out = []
        for word in text.split():
            kind, n = word.split(":")
            out.append((kind, l, st, int(n)))
        return out

    if st == C_:
        jobs = js("mod:0 mod:1 modT:0 mod:2 modT:1 mod:3 modT:2 mod:4 modT:3 rms:0 mod:5 modT:4 f1:0 mod:6 modT:5 f2:0 "
                  "mod:7 modT:6 f3:4 mod:8 modT:7 hf:4 mod:9 modT:8 mod:10 modT:9 mod:11 modT:10 modT:11")
        jobs += js("qk:0 vt:4 hs:0 hy:0 ko:0 hy:1 hy:2 hy:3 hy:4 hy:5 su:0 ut:0 su:1 qk:1 sp:0 hs:1 qk:2 hs:2 qk:3 sp:1 "
                   "hs:3 qk:4 df:4 hs:4 cv:0 cv:1")
    else:
        jobs = js("rms:0 f1:0 f2:0 f3:0 f3:1 f3:2 f3:3 hf:0 hf:1 hf:2 hf:3 "
                  "qk:0 vt:0 hs:0 vt:1 vt:2 rot:0 vt:3 hy:0 ck:0 hy:1 hy:2 hy:3 hy:4 hy:5 su:0 ut:0 su:1 ut:1 "
                  "qk:1 sp:0 hs:1 qk:2 rot:1 hs:2 qk:3 rot:2 hs:3 qk:4 rot:3 hs:4 sp:1 df:0 rot:4 df:1 df:2 df:3 cv:0 cv:1")
    jobs += attention_jobs(l, st)
    jobs += [("wo", l, st, j) for j in range(KC)] + [("rms", l, st, 1)] + [("wq", l, st, j) for j in range(KC)]
    jobs += [("tok", l, st, i) for i in range(2 * NT[st])]
    for i in range(2 * NT[st]):
        jobs += [("ka", l, st, i), ("kb", l, st, i)]
        jobs += start_jobs(phase(l, st)) if i == 1 and (st == L_ or l == 0) else []
    return jobs


ROOM = {"mod": 68, "modT": 8, "rms": 20, "f1": 10, "f2": 10, "f3": 10, "hf": 30, "qk": 48, "vt": 40, "hs": 5, "rot": 5,
        "ck": 2, "ko": 2, "hy": 38, "su": 53, "ut": 8, "sp": 5, "df": 12, "cv": 50, "as": 9, "at": 9, "av": 9, "wo": 53,
        "wq": 55, "tok": 6, "ka": 6, "kb": 6, "fence": 0, "stage": 0, "pick": 0, "gexp": 0}

GROUPS = ((0, C_), (0, L_), (1, C_), (1, L_))
UNITS = tuple(PEER_HEADS * NT[st] for _, st in GROUPS)
UNIT0 = tuple(sum(UNITS[:i]) for i in range(len(GROUPS)))
GROUP_TILE0 = tuple(u // PEER_HEADS for u in UNIT0)
PER_PIECE = 1
PIECES = TOPK // PER_PIECE
PICK_LINKS = (0, 5, 10, 16, 20, 23, 27)
PICK_PARTS = len(PICK_LINKS) - 1


def step_jobs(grp, u):
    n, jobs = UNITS[grp], []
    jobs += [("open", grp, u - 1, 0)] if u % PEER_HEADS == 1 else []
    jobs += [("stage", grp, u + 1, 0)] if u + 1 < n else []
    for p in range(PIECES):
        jobs += [("dot", grp, u, p)] if u < n else []
        jobs += [("add", grp, u - 1, p)] if u else []
        jobs += [("pick", grp, u + 1, p // 2)] if u + 1 < n and p % 2 and p // 2 < PICK_PARTS else []
    jobs += [("weigh", grp, u, 0)] if u < n else []
    jobs += [("gexp", grp, u + 1, 0)] if u + 1 < n else []
    jobs += [("close", grp, u - 1, 0)] if u and u % PEER_HEADS == 0 else []
    return jobs


def expert_jobs(grp, steps):
    return [job for u in steps for job in step_jobs(grp, u)]


def start_jobs(grp):
    return [("stage", grp, 0, 0)] + [("pick", grp, 0, p) for p in range(PICK_PARTS)] + [("gexp", grp, 0, 0)]


def weave(mixer, experts):
    total, cost, taken, out = sum(ROOM[j[0]] for j in mixer), 0, 0, []
    for job in mixer:
        out.append(job)
        cost += ROOM[job[0]]
        upto = min(len(experts), len(experts) * cost // total)
        out += experts[taken:upto]
        taken = upto
    return out + experts[taken:]


LOOP = "loop"
ORDER = mixer_jobs(0, C_)
for _l in range(DEPTH):
    _c, _g = 2 * _l, 2 * _l + 1
    ORDER += weave(mixer_jobs(_l, L_), expert_jobs(_c, range(UNITS[_c] + 1)))
    if _l + 1 < DEPTH:
        _a = 2
        ORDER += weave(mixer_jobs(_l + 1, C_), expert_jobs(_g, range(PEER_HEADS * _a + 1)))
    else:
        _a = 0
        ORDER += expert_jobs(_g, range(1))
    ORDER += [(LOOP, _g, _a, LAT_TILES - 1)]
    ORDER += expert_jobs(_g, range(PEER_HEADS * (LAT_TILES - 1) + 1, UNITS[_g] + 1))
    if _l + 1 < DEPTH:
        ORDER += start_jobs(_g + 1)


def loop_steps(grp, t):
    for kind, _, u, n in expert_jobs(grp, range(PEER_HEADS + 1, 2 * PEER_HEADS + 1)):
        yield kind, (t - 1) * PEER_HEADS + u, u, n


NUMBER, _count = {}, {}
for _job in ORDER:
    NUMBER[_job] = _count.get(_job[0], 0)
    _count[_job[0]] = NUMBER[_job] + 1


def done(*job):
    return NUMBER[job] + 1


READ = {"rms": "stat_read", "mod": "modrow_ready", "modT": "mod_ready", "f1": "arg_ready", "f2": "arg_ready",
        "f3": "ab_ready", "hf": "filt_ready", "qk": "qg_ready", "vt": "vt_read", "hs": "hs_read", "rot": "rot_ready",
        "hy": "hy_read", "ck": "ck_ready", "ko": "ko_ready", "su": "su_ready", "ut": "ut_ready", "sp": "sp_ready",
        "df": "y_ready", "cv": "cv_ready", "wo": "x_ready", "wq": "pq_ready", "tok": "tok_ready", "ka": "key0_read",
        "kb": "key1_read"}
BANKED = [j for j in ORDER if j[0] in READ]
BANK = {j: 2 + i % 6 for i, j in enumerate(BANKED)}
BANK_BEFORE = {j: BANKED[i - 6] for i, j in enumerate(BANKED) if i >= 6}


def read_value(job):
    kind, l, st, n = job
    return 2 * NUMBER[job] + (1 if kind == "f1" else 2) if kind in ("f1", "f2") else NUMBER[job] + 1


STREAM = []
for _l in range(DEPTH):
    for _st in (C_, L_):
        def _b(kind, i, sem, *job):
            STREAM.append(((kind, _l, _st, i), (sem, done(job[0], _l, _st, job[1]))))

        if _st == C_:
            for _i in range(24):
                _b("ada", _i, "mod_mm", "mod", _i // 2)
        else:
            for _i in range(2):
                _b("dft", _i, "hf_mm", "hf", 3)
        _last = TILE0[_st] + NT[_st] - 1
        for _i, _sem, *_job in ((0, "vt_mm", "vt", _last), (1, "vt_mm", "vt", _last), (2, "hy_mm", "hy", 1),
                                (3, "hy_mm", "hy", 3), (4, "hy_mm", "hy", 5), (5, "su_mm", "su", 1), (6, "qk_mm", "qk", 2),
                                (7, "qk_mm", "qk", 4)):
            _b("win", _i, _sem, *_job)
        if _st == L_:
            for _i in range(2):
                _b("dftu", _i, "df_mm", "df", 3)
            for _i in range(2, 4):
                _b("dftu", _i, "cv_mm", "cv", 1)
        for _i in range(4):
            _b("wout", _i, "wo_mm", "wo", 2 * _i + 1)
        for _i in range(4):
            _b("wq", _i, "wq_mm", "wq", 2 * _i + 1)
        _b("keys", 0, "kb_mm", "kb", 2 * NT[_st] - 1)
AT = {block: n for n, (block, _) in enumerate(STREAM)}


def mixer_peer_kernel(nc, xT_in, cT_in, cache_k, cache_v, ada, win, wout, wq, dft, dft_ctx, small, wide, decays,
                      fw12, featsT, sgw, keysT, rope, consts, peer_u, peer_v,
                      y_prompt, y_sample, new_k, new_v):
    with ExitStack() as ctx:
        def sb(name, cols, dt=F32, parts=P):
            return ctx.enter_context(nc.sbuf_tensor(name, [parts, cols], dt))

        def sem(name):
            return ctx.enter_context(nc.semaphore(name))

        def grid(x, rows):
            return x.rearrange("p (a b) -> p a b", a=rows)

        ring = sb("ring", SLOTS * BLOCK)
        rows_ring = sb("rows_ring", 2 * ROWS * D_MODEL)
        xT = grid(sb("xT", KC * TOK)[:, :], KC)
        mix = grid(sb("mix", KC * TOK)[:, :], KC)
        hT, filt, gate_u, kT, qT, probs, probsT, scores, h_tok, raw, uT, x0, sin_arg, sin_out, filt_ab = ([] for _ in range(15))
        for st in (L_, C_):
            w, nt = WIDTH[st], NT[st]
            n_scores = PEER_HEADS * nt * 2 * N_KEYS
            n_keys = PAST + LAT if st == L_ else CTX
            size = max(n_scores + nt * D_MODEL, (KC + 2 + 4) * w + nt * 512 + 3 * n_keys + max(2 * n_keys, 2 * w + 4))
            area = sb(f"area{st}", size)
            at = [0]

            def part(n):
                a = at[0]
                at[0] += n
                assert at[0] <= size
                return area[:, a:a + n]

            hT.append(grid(part(KC * w), KC))
            filt.append(part(nt * 512).rearrange("p (c r n) -> p c r n", c=nt, r=2))
            gate_u.append(grid(part(2 * w), 2))
            kT.append(part(n_keys))
            q = part(4 * w)
            qT.append(grid(q, 4))
            filt_ab.append(q.rearrange("p (t r n) -> p t r n", t=nt, r=2))
            a, b = part(max(2 * n_keys, 2 * w + 4)), part(2 * n_keys)
            probs.append(grid(a[:, 0:2 * n_keys], 2))
            probsT.append(grid(b, 2))
            raw.append(grid(a[:, 0:2 * w + 4], 2))
            uT.append(grid(a[:, 0:nt * HY_CH], nt))
            x0.append(grid(b[:, 0:2 * w], 2))
            sin_arg.append(grid(a[:, 0:2 * w], 2))
            sin_out.append(grid(b[:, 0:2 * w], 2))
            scores.append(area[:, 0:n_scores])
            h_tok.append(area[:, n_scores:n_scores + nt * D_MODEL])
        mod_row = mix[:, 0:2, 0:LAT]
        decay = mix[:, 2, 0:LAT]
        fw1 = mix[0:HY_EMB, 3, 0:HY_FFN]
        fw12_place = mix[0:HY_FFN, 3, 0:2 * HY_FFN]
        fw2 = mix[0:HY_FFN, 3, HY_FFN:2 * HY_FFN]
        fw3 = mix[0:HY_FFN, 4, 0:LAT]
        feats = (mix[0:HY_EMB, 5, 0:LAT], mix[0:HY_EMB, 3, P:2 * P])
        out_tok = (mix[:, 6:8, 0:LAT], mix[:, :, LAT:TOK])

        def out_chunk(st, k):
            return out_tok[L_][:, k // 4, k % 4 * P:k % 4 * P + P] if st == L_ else out_tok[C_][:, k, :]

        x1 = sb("x1", LAT)
        sg_v = grid(sb("sg_v", TILES * SG_W)[:, :], TILES)
        v_tok = grid(sb("v_tok", (TILES + 1) * P)[:, :], TILES + 1)
        rstd = sb("rstd", LAT)
        work = rstd[:, :]
        zeros = sb("zeros", P)
        tmp = grid(sb("tmp", 2 * LAT)[:, :], 2)
        k_past = sb("k_past", P)
        k_out = sb("k_out", P)
        sg_junk = sb("sg_junk", SG_W)
        sq = grid(sb("sq", 2 * LAT)[:, :], 2)
        ident = sb("ident", P)
        ones = sb("ones", P)
        head_ones = sb("head_ones", P)
        swap = sb("swap", P)
        tok_const = sb("tok_const", TILES + 1 + TOPK)
        neg_time = tok_const[:, 0:TILES]
        eps = tok_const[:, TILES:TILES + 1]
        iota16 = tok_const[:, TILES + 1:TILES + 1 + TOPK]
        cos_sin = grid(sb("cos_sin", 2 * LAT)[:, :], 2)
        dft128 = grid(sb("dft128", 4 * P)[:, :], 4)
        csil = grid(sb("csil", 2 * KC)[:, :], KC)
        par = sb("par", S_COLS)
        widep = sb("widep", SG_W + 2 * P)
        sg_gain = widep[:, 0:SG_W]
        sg_bias = grid(widep[:, SG_W:SG_W + 2 * P], 2)
        sgwT = grid(sb("sgwT", 4 * P)[:, :], 4)
        modTs = [grid(sb(f"modT{i}", 6 * KC * 2)[:, :], 6 * KC) for i in range(2)]
        SH_M, SC_M, G_M, SH_F, SC_F, G_F = range(0, 6 * KC, KC)
        small8 = sb("small8", 64)
        ssq = small8[:, 0:5]
        sg_rstd = small8[:, 8:13]
        negmax = small8[:, 16:18]
        rowsum = small8[:, 18:20]
        rinv = small8[:, 20:22]
        topv = grid(sb("topv", 2 * TOPK)[:, :], 2)
        topi = grid(sb("topi", 2 * TOPK, U32)[:, :], 2)
        topf = grid(sb("topf", 2 * TOPK)[:, :], 2)
        best = sb("best", TOPK)
        pos = sb("pos", TOPK, U32)
        posij = grid(sb("posij", 2 * TOPK, U32)[:, :], 2)
        posf = grid(sb("posf", 2 * TOPK)[:, :], 2)
        picked = grid(sb("picked", 2 * TOPK)[:, :], 2)
        idxf = sb("idxf", TOPK)
        idx = [sb(f"idx{b}", TOPK, U32) for b in range(IDX_PLACES)]
        gate_e = sb("gate_e", TOPK)
        gate_s = sb("gate_s", 4)
        dots = sb("dots", TOPK)
        acts = sb("acts", TOPK)
        wts = sb("wts", TOPK)
        unit_cols = sb("unit_s", 2 * N_KEYS)
        unit_s = grid(unit_cols[:, :], 2)
        cand = sb("cand", TOPK * TOPK)
        onehot = sb("onehot", TOPK * TOPK)
        diag = grid(sb("diag", 4 * P)[:, :], 4)
        softmax_diag = grid(sg_junk[:, :], 2)
        psum_cols = ctx.enter_context(nc.psum_tensor("psum", [P, 8 * 512], F32))
        psum = grid(psum_cols[:, :], 8)
        acc = psum[:, 0:2, :]
        acc8 = grid(psum_cols[:, 0:D_MODEL], KC)

        def slot(n):
            return ring[:, (n % SLOTS) * BLOCK:(n % SLOTS + 1) * BLOCK]

        def row(table, k):
            return rows_ring[:, (table * ROWS + k % ROWS) * D_MODEL:(table * ROWS + k % ROWS + 1) * D_MODEL]

        names = """first_loaded const_loaded silu_ready zero_ready small_loaded cache_loaded cache_stored
        sq_ready sq_used stat_read rstd_ready xn_ready h_ready
        mod_mm modrow_ready modT_mm mod_ready scale_ready
        filt_mm f3_mm arg_ready sin_ready env_ready ab_ready hf_mm filt_ready
        qk_mm hsq_ready qg_ready hs_mm hs_read hr_ready qn_ready rot_mm rot_ready
        vt_mm vt_read sgr_ready sgn_ready su_mm su_ready sp_mm sp_ready
        hy_mm hy_read hy_conv gu_ready ut_mm ut_ready df_mm y_ready cv_mm cv_ready
        ck_mm ck_ready ko_mm ko_ready
        sc_mm max_ready exp_ready probs_ready pt_mm pt_ready pv_mm attn_ready
        wo_mm x_ready wq_mm pq_ready tok_mm tok_ready ka_mm kb_mm key0_read key1_read
        staged idx_ready best_ready gexp_ready
        u_free gelu_ready w_ready diag_ready v_free acc_mm acc_read back_mm x_added
        dve_link act_link pads_ready wlink topk_link pool_tick dve_tick y_mm y_copied""".split()
        s = {n: sem(n) for n in names}
        y_stored = [sem("y_stored0"), sem("y_stored1")]
        landed = [sem(f"landed{k}") for k in range(SLOTS)]
        row_landed = [[sem(f"{name}_landed{k}") for k in range(ROWS)] for name in ("down", "up")]

        def qk_dst(st, n):
            if n:
                return qT[st][:, n - 1, :]
            return kT[L_][:, PAST:PAST + LAT] if st == L_ else kT[C_]

        def unit_of(st, n):
            c, half, t = n // (2 * NT[st]), n // NT[st] % 2, n % NT[st]
            return c, slice(64 * half, 64 * half + 64), t

        def att_bank(st, n):
            if st == C_:
                return psum_cols[:, 512 * (2 + n % 3):512 * (3 + n % 3)]
            return psum_cols[:, 1024 * (1 + n % 3):1024 * (2 + n % 3)]

        def out_bank(st, c):
            return psum[:, (0 if st == L_ else 6) + c % 2, :]

        def key_dst(st, i, half):
            return scores[st].rearrange("p (u h n) -> p u h n", h=2, n=N_KEYS)[:, 4 * i:4 * i + 4, half, :]

        KEYS = (PAST + LAT, CTX)
        HY_CHUNK = (2, 4, 3, 5, 0, 1)

        def hy_dst(st, i):
            return (x1[:, 0:WIDTH[st]], gate_u[st][:, 0, :], x1[:, 0:WIDTH[st]], gate_u[st][:, 1, :],
                    x0[st][:, 0, :], x0[st][:, 1, :])[i]

        def tile_of(grp, u):
            return GROUP_TILE0[grp] + u // PEER_HEADS

        def latent_unit(grp, g):
            return g - (GROUPS[grp][0] + 1) * PEER_HEADS

        def latent_tile(grp, tile):
            return tile - (GROUPS[grp][0] + 1)

        TOPK_LINKS = PICK_LINKS[-1]
        STEPS_BEFORE_PLAIN = (10, *range(16, TOPK_LINKS + 1))
        block = ctx.enter_context(nc.Block())

        @block.sync
        def _(sp):
            for dst, src in ((csil, cT_in), (ident[:], consts[0])):
                sp.dma_start(dst, src).then_inc(s["first_loaded"], 16)

            def const_loads():
                for dst, src in ((xT, xT_in), (ones[:], consts[1]), (head_ones[:], consts[2]), (swap[:], consts[3]),
                                 (cos_sin, rope), (dft128, dft_ctx), (tok_const[:], consts[4][:, 0:TILES + 1 + TOPK])):
                    sp.dma_start(dst, src).then_inc(s["const_loaded"], 16)

            def small_loads(l):
                if l:
                    sp.wait_ge(s["kb_mm"], done("kb", l - 1, L_, 2 * LAT_TILES - 1))
                    sp.wait_ge(s["cv_ready"], done("cv", l - 1, L_, 1))
                for dst, src in ((par[:], small[l]), (widep[:], wide[l]), (decay, decays[l]),
                                 (fw12_place, fw12[l][:, 0:2 * HY_FFN]), (fw3, fw12[l][:, 2 * HY_FFN:]), (sgwT, sgw[l]),
                                 (feats[C_], featsT[:, LAT:TOK]), (feats[L_], featsT[:, 0:LAT])):
                    sp.dma_start(dst, src).then_inc(s["small_loaded"], 16)
                sp.dma_start(k_past[:], cache_k[l]).then_inc(s["cache_loaded"], 16)
                sp.dma_start(v_tok[:, TILES, :], cache_v[l]).then_inc(s["cache_loaded"], 16)

            for n, ((kind, l, st, i), _) in enumerate(STREAM):
                if (kind, st, i) == ("ada", C_, 0) and l:
                    small_loads(l)
                if n == SLOTS:
                    small_loads(0)
                    const_loads()
                if n >= SLOTS:
                    name, value = STREAM[n - SLOTS][1]
                    sp.wait_ge(s[name], value)
                if kind == "keys":
                    sp.dma_start(slot(n)[:, 0:PEER_HEADS * N_KEYS], keysT[l]).then_inc(landed[n % SLOTS], 16)
                else:
                    src = dft[i] if kind in ("dft", "dftu") else {"ada": ada, "win": win, "wout": wout, "wq": wq}[kind][l][i]
                    sp.dma_start(slot(n), src).then_inc(landed[n % SLOTS], 16)
                if (kind, st, i) == ("wout", C_, 3):
                    sp.wait_ge(s["ko_ready"], l + 1)
                    sp.dma_start(new_k[l], k_out[:]).then_inc(s["cache_stored"], 16)
                    sp.wait_ge(s["vt_read"], done("vt", l, C_, LAT_TILES))
                    sp.dma_start(new_v[l], v_tok[:, LAT_TILES, :]).then_inc(s["cache_stored"], 16)
            sp.wait_ge(s["cache_stored"], 32 * DEPTH)
            for t in range(TILES):
                sp.wait_ge(s["y_copied"], t + 1)
                dst = y_sample[t * P:(t + 1) * P, :] if t < LAT_TILES else y_prompt
                sp.dma_start(dst, row(0, t % 2)).then_inc(y_stored[t % 2], 16)
            sp.wait_ge(y_stored[0], 16 * 3)
            sp.wait_ge(y_stored[1], 16 * 2)

        @block.gpsimd
        def _(pool):
            def fetch(table, grp, u, n, k):
                pool.wait_ge(s[("u_free", "v_free")[table]], (u + UNIT0[grp]) * TOPK + k + 1)
                pool.sem_inc(s["pool_tick"], 1)
                pool.indirect_dma_start(row(table, k), None, (peer_u, peer_v)[table],
                                        bass.IndirectOffsetOnAxis(ap=idx[n][:, k:k + 1], axis=0)
                                        ).then_inc(row_landed[table][k % ROWS], 16)

            def step(grp, u, n):
                known = isinstance(u, int)
                if not known or u < UNITS[grp]:
                    pool.wait_ge(s["idx_ready"], u + UNIT0[grp] + 1)
                for k in range(TOPK):
                    if not known or u < UNITS[grp]:
                        fetch(0, grp, u, n % IDX_PLACES, k)
                    if not known or u > 0:
                        fetch(1, grp, u - 1, (n - 1) % IDX_PLACES, k)

            pool.sem_inc(s["u_free"], ROWS)
            pool.sem_inc(s["v_free"], ROWS)
            for grp in range(len(GROUPS)):
                step(grp, 0, 0)
                with pool.Fori(0, UNITS[grp] // IDX_PLACES - 1) as four:
                    for n in range(1, IDX_PLACES + 1):
                        step(grp, four * IDX_PLACES + n, n)
                for u in range(UNITS[grp] - IDX_PLACES + 1, UNITS[grp] + 1):
                    step(grp, u, u)
            for table in range(2):
                for k in range(ROWS):
                    pool.wait_ge(row_landed[table][k], 16 * (TOPK // ROWS) * sum(UNITS))

        def row_value(g, k):
            return g * (16 * (TOPK // ROWS)) + 16 * (k // ROWS + 1)

        @block.tensor
        def _(pe):
            def blk(kind, l, st, i):
                n = AT[kind, l, st, i]
                pe.wait_ge(landed[n % SLOTS], 16 * (n // SLOTS + 1))
                return slot(n)

            def rms(l, st, i, g):
                first, w = KC * NUMBER["rms", l, st, i], WIDTH[st]
                if first == 0:
                    pe.wait_ge(s["const_loaded"], 16 * CONST_LOADS)
                for k in range(KC):
                    pe.wait_ge(s["sq_ready"], first + k + 1)
                    pe.matmul(g[:, 0:w], ones[:], sq[:, k % 2, 0:w], start=(k == 0), stop=(k == KC - 1)).then_inc(s["sq_used"], 1)

            def mod(l, st, n, g):
                for half in range(2):
                    w = blk("ada", l, st, 2 * n + half)
                    for j in range(4):
                        m = pe.matmul(g[0:2, 0:512], csil[:, 4 * half + j, :], w[:, j * 512:(j + 1) * 512],
                                      start=(half == 0 and j == 0), stop=(half == 1 and j == 3))
                m.then_inc(s["mod_mm"], 1)

            def modT(l, st, n, g):
                pe.wait_ge(s["modrow_ready"], done("mod", l, st, n))
                for j in range(4):
                    m = pe.transpose(g[:, 2 * j:2 * j + 2], mod_row[0:2, n % 2, j * P:(j + 1) * P], ident[0:2, 0:2])
                m.then_inc(s["modT_mm"], 1)

            def f1(l, st, n, g):
                pe.wait_ge(s["small_loaded"], 16 * SMALL_LOADS * (l + 1))
                pe.matmul(g[0:HY_FFN, 0:WIDTH[st]], fw1, feats[st], start=True, stop=True).then_inc(s["filt_mm"], 1)

            def f2(l, st, n, g):
                pe.wait_ge(s["sin_ready"], 2 * phase(l, st) + 1)
                pe.matmul(g[0:HY_FFN, 0:WIDTH[st]], fw2, sin_out[st][0:HY_FFN, 0, :], start=True, stop=True).then_inc(s["filt_mm"], 1)

            def f3(l, st, t, g):
                pe.wait_ge(s["sin_ready"], 2 * phase(l, st) + 2)
                pe.matmul(g, sin_out[st][0:HY_FFN, 1, (t - TILE0[st]) * P:(t - TILE0[st] + 1) * P], fw3, start=True, stop=True).then_inc(s["f3_mm"], 1)

            def spectrum(l, st, c, g, src, kind):
                for r in range(2):
                    out = g[:, r * HY_CH:(r + 1) * HY_CH]
                    if st == C_:
                        m = pe.matmul(out, dft128[:, r, :], src(0, r), start=True, stop=True)
                    else:
                        w = blk(kind, l, st, r)
                        for t in range(LAT_TILES):
                            m = pe.matmul(out, w[:, t * LAT + c * P:t * LAT + (c + 1) * P], src(t, r),
                                          start=(t == 0), stop=(t == LAT_TILES - 1))
                return m

            def hf(l, st, c, g):
                pe.wait_ge(s["ab_ready"], done("f3", l, st, TILE0[st] + NT[st] - 1))
                spectrum(l, st, c, g, lambda t, r: filt_ab[st][:, t, r, :], "dft").then_inc(s["hf_mm"], 1)

            def project(st, w, g, src, ready=None, first=0):
                for k in range(KC):
                    if ready:
                        pe.wait_ge(s[ready], first + k + 1)
                    m = pe.matmul(g[:, 0:WIDTH[st]], w[:, k * P:(k + 1) * P], src(k), start=(k == 0), stop=(k == KC - 1))
                return m

            def half_of(w, half):
                return w[:, half * 1024:(half + 1) * 1024]

            def from_h(st):
                return lambda k: hT[st][:, k, :]

            def from_mix(st):
                return lambda k: mix[:, k, COLS[st]]

            def qk(l, st, n, g):
                w = half_of(blk("win", l, st, 0), 0) if n == 0 else half_of(blk("win", l, st, 6 + (n - 1) // 2), (n - 1) % 2)
                project(st, w, g, from_h(st), "h_ready", KC * NUMBER["rms", l, st, 0]).then_inc(s["qk_mm"], 1)

            def vt(l, st, t, g):
                w0 = half_of(blk("win", l, st, 0), 1)
                w1 = blk("win", l, st, 1)
                a = (t - TILE0[st]) * P
                for k in range(KC):
                    x = hT[st][:, k, a:a + P]
                    pe.matmul(g[:, 0:P], x, w0[:, k * P:(k + 1) * P], start=(k == 0), stop=(k == KC - 1))
                for k in range(KC):
                    x = hT[st][:, k, a:a + P]
                    m = pe.matmul(g[:, P:3 * P], x, w1.rearrange("p (c k n) -> p c k n", c=2, k=KC)[:, :, k, :],
                                  start=(k == 0), stop=(k == KC - 1))
                m.then_inc(s["vt_mm"], 1)

            def hs(l, st, n, g):
                pe.wait_ge(s["hsq_ready"], done("qk", l, st, n))
                pe.matmul(g[:, 0:WIDTH[st]], head_ones[:], sq[:, n % 2, 0:WIDTH[st]], start=True, stop=True).then_inc(s["hs_mm"], 1)

            def rot(l, st, n, g):
                pe.wait_ge(s["qn_ready"], done("hs", l, st, n))
                pe.matmul(g, swap[:], qk_dst(st, n), start=True, stop=True).then_inc(s["rot_mm"], 1)

            def ck(l, st, n, g):
                pe.wait_ge(s["cache_loaded"], 32 * (l + 1))
                pe.transpose(g[:, 0:P], k_past[:], ident[:]).then_inc(s["ck_mm"], 1)

            def ko(l, st, n, g):
                pe.wait_ge(s["qn_ready"], done("hs", l, C_, 0))
                pe.transpose(g[:, 0:P], kT[C_], ident[:]).then_inc(s["ko_mm"], 1)

            def hy(l, st, i, g):
                project(st, half_of(blk("win", l, st, 2 + i // 2), i % 2), g, from_h(st)).then_inc(s["hy_mm"], 1)

            def su(l, st, j, g):
                project(st, half_of(blk("win", l, st, 5), j), g, from_h(st)).then_inc(s["su_mm"], 1)

            def ut(l, st, n, g):
                pe.wait_ge(s["gu_ready"], 2 * phase(l, st) + 2)
                for i in range(min(2, NT[st])):
                    t = 2 * n + i
                    for j in range(2):
                        m = pe.transpose(g[:, (2 * i + j) * P:(2 * i + j + 1) * P], gate_u[st][:, j, t * P:(t + 1) * P], ident[:])
                m.then_inc(s["ut_mm"], 1)

            def sp_(l, st, j, g):
                pe.wait_ge(s["sgn_ready"], done("vt", l, st, TILE0[st] + NT[st] - 1))
                for t in range(NT[st]):
                    for half in range(2):
                        m = pe.matmul(g[64 * half:64 * half + 64, t * P:(t + 1) * P],
                                      sg_v[:, TILE0[st] + t, j * P + 64 * half:j * P + 64 * half + 64], sgwT[:, 2 * j + half, :],
                                      start=True, stop=True)
                m.then_inc(s["sp_mm"], 1)

            def df(l, st, c, g):
                pe.wait_ge(s["ut_ready"], done("ut", l, st, NT[st] // 2 - 1 if st == L_ else 0))
                spectrum(l, st, c, g, lambda t, r: uT[st][:, t, :], "dftu").then_inc(s["df_mm"], 1)

            def cv(l, st, j, g):
                pe.wait_ge(s["y_ready"], done("df", l, st, TILE0[st] + NT[st] - 1))
                if st == L_:
                    ws = [blk("dftu", l, st, 2 + r) for r in range(2)]
                    wave = lambda r, c: ws[r][:, c * LAT:(c + 1) * LAT]
                else:
                    wave = lambda r, c: dft128[:, 2 + r, :]
                for c in range(NT[st]):
                    for r in range(2):
                        m = pe.matmul(g[:, 0:WIDTH[st]], filt[st][:, c, r, j * P:(j + 1) * P], wave(r, c),
                                      start=(c == 0 and r == 0), stop=(c == NT[st] - 1 and r == 1))
                m.then_inc(s["cv_mm"], 1)

            def fence(l, st, n):
                if n == 0:
                    first = BANKED.index(("cv", l, st, 1)) + 1
                    for job in BANKED[first - 6:first]:
                        pe.wait_ge(s[READ[job[0]]], read_value(job))
                    if st == L_:
                        pe.wait_ge(s["rot_ready"], done("rot", l, st, 4))
                        pe.wait_ge(s["ck_ready"], l + 1)
                    else:
                        pe.wait_ge(s["qn_ready"], done("hs", l, st, 4))
                else:
                    pe.wait_ge(s["attn_ready"], 4 * phase(l, st) + 4)
                    pe.wait_ge(s["sp_ready"], done("sp", l, st, 1))
                    pe.wait_ge(s["cv_ready"], done("cv", l, st, 1))

            def att_scores(l, st, n):
                c, rows, t = unit_of(st, n)
                if n >= 3:
                    pe.wait_ge(s["pt_ready"], done("at", l, st, n - 3))
                g = att_bank(st, n)
                q = qT[st][rows, c, t * P:(t + 1) * P]
                if st == L_:
                    pe.matmul(g[:, 0:512], q, kT[st][rows, 0:512], start=True, stop=True)
                    m = pe.matmul(g[:, 512:TOK], q, kT[st][rows, 512:TOK], start=True, stop=True)
                else:
                    m = pe.matmul(g[:, 0:CTX], q, kT[st][rows, :], start=True, stop=True)
                m.then_inc(s["sc_mm"], 1)

            def att_transpose(l, st, n):
                pe.wait_ge(s["probs_ready"], done("at", l, st, n))
                for b in range(KEYS[st] // P):
                    m = pe.matmul(att_bank(st, n)[:, b * P:(b + 1) * P], probs[st][:, n % 2, b * P:(b + 1) * P],
                                  softmax_diag[:, n % 2, :], start=True, stop=True)
                m.then_inc(s["pt_mm"], 1)

            def att_values(l, st, n):
                c, rows, t = unit_of(st, n)
                pe.wait_ge(s["pt_ready"], done("at", l, st, n))
                if n % (2 * NT[st]) == 0 and c >= 2:
                    pe.wait_ge(s["attn_ready"], 4 * phase(l, st) + c - 1)
                blocks = [TILES, 0, 1, 2, 3] if st == L_ else [LAT_TILES]
                for i, b in enumerate(blocks):
                    m = pe.matmul(out_bank(st, c)[rows, t * P:(t + 1) * P], v_tok[:, b, rows], probsT[st][:, n % 2, i * P:(i + 1) * P],
                                  start=(i == 0), stop=(i == len(blocks) - 1))
                m.then_inc(s["pv_mm"], 1)

            def wo(l, st, j, g):
                project(st, half_of(blk("wout", l, st, j // 2), j % 2), g, from_mix(st)).then_inc(s["wo_mm"], 1)

            def wq_(l, st, j, g):
                project(st, half_of(blk("wq", l, st, j // 2), j % 2), g, from_h(st), "h_ready",
                        KC * NUMBER["rms", l, st, 1]).then_inc(s["wq_mm"], 1)

            def tok(l, st, i, g):
                t, half = i // 2, i % 2
                for k in range(4):
                    m = pe.transpose(g[:, k * P:(k + 1) * P], hT[st][:, 4 * half + k, t * P:(t + 1) * P], ident[:])
                m.then_inc(s["tok_mm"], 1)

            def key(l, st, i, g, half):
                t, h0 = i // 2, 4 * (i % 2)
                if i == 0 and half == 0:
                    pe.wait_ge(s["tok_ready"], done("tok", l, st, 2 * NT[st] - 1))
                    pe.wait_ge(s["pq_ready"], done("wq", l, st, KC - 1))
                keys = grid(blk("keys", l, st, 0)[:, 0:PEER_HEADS * N_KEYS], PEER_HEADS)
                a = COLS[st].start + t * P
                rows = slice(64 * half, 64 * half + 64)
                for h in range(4):
                    m = pe.matmul(g[:, h * P:(h + 1) * P], mix[rows, h0 + h, a:a + P], keys[rows, h0 + h, :],
                                  start=True, stop=True)
                m.then_inc(s[("ka_mm", "kb_mm")[half]], 1)

            def open_tile(grp, tile):
                for b in range(2):
                    pe.matmul(acc[:, b, :], zeros[:], cos_sin[:, 0, :], start=True, stop=False)

            def add(grp, g, p):
                for k in range(PER_PIECE * p, PER_PIECE * (p + 1)):
                    pe.wait_ge(row_landed[1][k % ROWS], row_value(g, k))
                    pe.wait_ge(s["diag_ready"], latent_unit(grp, g) * TOPK + k + 1)
                    for b in range(2):
                        m = pe.matmul(acc[:, b, :], diag[:, k % 4, :], row(1, k)[:, b * 512:(b + 1) * 512], start=False, stop=False)
                    m.then_inc(s["v_free"], 1)

            def close_tile(grp, tile):
                if GROUPS[grp][1] == L_:
                    for b in range(2):
                        m = pe.matmul(acc[:, b, :], zeros[:], cos_sin[:, 0, :], start=False, stop=True)
                    m.then_inc(s["acc_mm"], 1)
                    pe.wait_ge(s["acc_read"], latent_tile(grp, tile) + 1)
                else:
                    pe.wait_ge(s["v_free"], (tile + 1) * PEER_HEADS * TOPK + ROWS)
                for k in range(KC):
                    m = pe.transpose(acc[:, k // 4, k % 4 * P:k % 4 * P + P], out_chunk(GROUPS[grp][1], k), ident[:])
                m.then_inc(s["back_mm"], 1)
                pe.wait_ge(s["x_added"], tile + 1)

            mixers = {"rms": rms, "mod": mod, "modT": modT, "f1": f1, "f2": f2, "f3": f3, "hf": hf, "qk": qk, "vt": vt,
                      "hs": hs, "rot": rot, "ck": ck, "ko": ko, "hy": hy, "su": su, "ut": ut, "sp": sp_, "df": df, "cv": cv,
                      "wo": wo, "wq": wq_, "tok": tok, "ka": lambda *a: key(*a, 0), "kb": lambda *a: key(*a, 1)}
            unbanked = {"fence": fence, "as": att_scores, "at": att_transpose, "av": att_values}

            pe.wait_ge(s["first_loaded"], 32)
            pe.wait_ge(s["silu_ready"], 1)
            pe.wait_ge(s["zero_ready"], 1)
            for job in ORDER:
                kind, a, b, n = job
                if kind in mixers:
                    before = BANK_BEFORE.get(job)
                    if before:
                        pe.wait_ge(s[READ[before[0]]], read_value(before))
                    mixers[kind](a, b, n, psum[:, BANK[job], :])
                elif kind in unbanked:
                    unbanked[kind](a, b, n)
                elif kind == "open":
                    if GROUPS[a][1] == L_:
                        open_tile(a, tile_of(a, b))
                elif kind == "add":
                    if GROUPS[a][1] == L_:
                        add(a, UNIT0[a] + b, n)
                elif kind == "close":
                    close_tile(a, tile_of(a, b))
                elif kind == LOOP:
                    with pe.Fori(b, n) as t:
                        for kind, u, m, p in loop_steps(a, t):
                            if kind == "open":
                                open_tile(a, t + GROUP_TILE0[a])
                            elif kind == "add":
                                add(a, u + UNIT0[a], p)
                            elif kind == "close":
                                close_tile(a, t + GROUP_TILE0[a])
            for t in range(TILES):
                if t >= 4:
                    pe.wait_ge(s["y_copied"], t - 3)
                for k in range(KC):
                    m = pe.transpose(psum[:, 2 * (t % 4) + k // 4, k % 4 * P:k % 4 * P + P], xT[:, k, t * P:(t + 1) * P], ident[:])
                m.then_inc(s["y_mm"], 1)

        @block.scalar
        def _(act):
            n_link = [0]

            def link(ins):
                n_link[0] += 1
                ins.then_inc(s["act_link"], 1)
                act.wait_ge(s["act_link"], n_link[0])

            def rms(l, st, i, g):
                q, w = NUMBER["rms", l, st, i], WIDTH[st]
                first = KC * q
                if first == 0:
                    act.wait_ge(s["const_loaded"], 16 * CONST_LOADS)
                if i == 0 and l:
                    act.wait_ge(s["x_added"], GROUP_TILE0[phase(l - 1, st)] + NT[st])
                for k in range(KC):
                    if i:
                        act.wait_ge(s["x_ready"], done("wo", l, st, k))
                    if first + k >= 2:
                        act.wait_ge(s["sq_used"], first + k - 1)
                    act.activation(sq[:, k % 2, 0:w], xT[:, k, COLS[st]], ACT.Square).then_inc(s["sq_ready"], 1)
                act.wait_ge(s["sq_used"], first + KC)
                act.activation(rstd[:, 0:w], g[:, 0:w], ACT.Ln, bias=eps).then_inc(s["stat_read"], 1)
                act.wait_ge(s["stat_read"], q + 1)
                act.activation(rstd[:, 0:w], rstd[:, 0:w], ACT.Exp, scale=-0.5).then_inc(s["rstd_ready"], 1)
                shift, scale = ((SH_M, SC_M), (SH_F, SC_F))[i]
                act.wait_ge(s["scale_ready"], 2 * l + i + 1)
                for k in range(KC):
                    act.wait_ge(s["xn_ready"], first + k + 1)
                    act.activation(hT[st][:, k, :], hT[st][:, k, :], ACT.Identity, bias=modTs[l % 2][:, shift + k, st:st + 1],
                                   scale=modTs[l % 2][:, scale + k, st:st + 1]).then_inc(s["h_ready"], 1)

            def mod(l, st, n, g):
                q = NUMBER["mod", l, st, n]
                act.wait_ge(s["mod_mm"], q + 1)
                if q >= 2:
                    act.wait_ge(s["modT_mm"], q - 1)
                act.copy(mod_row[0:2, n % 2, :], g[0:2, :]).then_inc(s["modrow_ready"], 1)

            def sine(l, st, i):
                act.wait_ge(s["arg_ready"], 2 * phase(l, st) + i + 1)
                act.activation(sin_out[st][0:HY_FFN, i, :], sin_arg[st][0:HY_FFN, 0, :], ACT.Sin).then_inc(s["sin_ready"], 1)

            def f3(l, st, t, g):
                q = NUMBER["f3", l, st, t]
                if st == C_:
                    act.wait_ge(s["small_loaded"], 16 * SMALL_LOADS * (l + 1))
                    link(act.activation(decay, decay, ACT.Abs))
                if q >= 2:
                    act.wait_ge(s["ab_ready"], q - 1)
                act.activation(tmp[:, q % 2, :], decay, ACT.Exp, scale=neg_time[:, t:t + 1]).then_inc(s["env_ready"], 1)

            def hf(l, st, c, g):
                act.wait_ge(s["hf_mm"], done("hf", l, st, c))
                act.copy(filt[st][:, c - TILE0[st], :, :].rearrange("p r n -> p (r n)"), g).then_inc(s["filt_ready"], 1)

            def qk(l, st, n, g):
                act.wait_ge(s["qk_mm"], done("qk", l, st, n))
                if n >= 2:
                    act.wait_ge(s["hs_mm"], done("hs", l, st, n - 2))
                act.activation(sq[:, n % 2, 0:WIDTH[st]], g[:, 0:WIDTH[st]], ACT.Square).then_inc(s["hsq_ready"], 1)

            def hs(l, st, n, g):
                w = WIDTH[st]
                act.wait_ge(s["hs_mm"], done("hs", l, st, n))
                if n >= 2:
                    act.wait_ge(s["qn_ready"], done("hs", l, st, n - 2))
                act.activation(tmp[:, n % 2, 0:w], g[:, 0:w], ACT.Ln, bias=eps).then_inc(s["hs_read"], 1)
                act.wait_ge(s["hs_read"], done("hs", l, st, n))
                act.activation(tmp[:, n % 2, 0:w], tmp[:, n % 2, 0:w], ACT.Exp, scale=-0.5).then_inc(s["hr_ready"], 1)

            def vt(l, st, t, g):
                act.wait_ge(s["vt_mm"], done("vt", l, st, t))
                if st == C_ and l:
                    act.wait_ge(s["cache_stored"], 32 * l)
                act.copy(v_tok[:, t, :], g[:, 0:P])
                act.activation(sg_v[:, t, :], g[:, P:P + SG_W], ACT.Gelu_apprx_tanh).then_inc(s["vt_read"], 1)
                if t == TILE0[st] + NT[st] - 1:
                    act.wait_ge(s["vt_read"], done("vt", l, st, t))
                    a, b = TILE0[st], TILE0[st] + NT[st]
                    for i in range(a, b):
                        link(act.activation(sg_junk[:], sg_v[:, i, :], ACT.Square, accum_out=ssq[:, i:i + 1]))
                    link(act.activation(sg_rstd[:, a:b], ssq[:, a:b], ACT.Ln, bias=eps, scale=1.0 / SG_W))
                    act.activation(sg_rstd[:, a:b], sg_rstd[:, a:b], ACT.Exp, scale=-0.5).then_inc(s["sgr_ready"], 1)

            def ko(l, st, n, g):
                act.wait_ge(s["ko_mm"], l + 1)
                act.copy(k_out[:], g[:, 0:P]).then_inc(s["ko_ready"], 1)

            def hy(l, st, i, g):
                ph, w = phase(l, st), WIDTH[st]
                act.wait_ge(s["hy_mm"], done("hy", l, st, i))
                if i == 0:
                    act.wait_ge(s["pads_ready"], ph + 1)
                if i >= 2:
                    act.wait_ge(s["hy_conv"], 6 * ph + i - 1)
                if i == 2:
                    act.wait_ge(s["gu_ready"], 2 * ph + 1)
                cc = HY_CHUNK[i]
                act.copy(raw[st][:, i % 2, 1:1 + w], g[:, 0:w])
                act.activation(hy_dst(st, i), g[:, 0:w], ACT.Identity, bias=par[:, S_CONVB + cc:S_CONVB + cc + 1],
                               scale=par[:, S_CONVW + 6 + cc:S_CONVW + 6 + cc + 1]).then_inc(s["hy_read"], 1)

            def su(l, st, j, g):
                act.wait_ge(s["su_mm"], done("su", l, st, j))
                act.activation(mix[:, 6 + j, COLS[st]], g[:, 0:WIDTH[st]], ACT.Gelu_apprx_tanh).then_inc(s["su_ready"], 1)

            def ut(l, st, n, g):
                act.wait_ge(s["ut_mm"], done("ut", l, st, n))
                act.wait_ge(s["hy_conv"], 6 * phase(l, st) + 6)
                k = min(2, NT[st])
                act.copy(uT[st][:, 2 * n:2 * n + k, :].rearrange("p t n -> p (t n)"), g[:, 0:k * HY_CH]).then_inc(s["ut_ready"], 1)

            def wq_(l, st, j, g):
                act.wait_ge(s["wq_mm"], done("wq", l, st, j))
                act.copy(mix[:, j, COLS[st]], g[:, 0:WIDTH[st]]).then_inc(s["pq_ready"], 1)

            def ka(l, st, i, g):
                act.wait_ge(s["ka_mm"], done("ka", l, st, i))
                act.copy(key_dst(st, i, 0), grid(g, 4)).then_inc(s["key0_read"], 1)

            jobs = {"rms": rms, "mod": mod, "f1": lambda l, st, n, g: sine(l, st, 0), "f2": lambda l, st, n, g: sine(l, st, 1),
                    "f3": f3, "hf": hf, "qk": qk, "hs": hs, "vt": vt, "ko": ko, "hy": hy, "su": su, "ut": ut, "wq": wq_, "ka": ka}

            def att_exp(l, st, n):
                act.wait_ge(s["max_ready"], done("as", l, st, n))
                act.activation(probs[st][:, n % 2, :], att_bank(st, n)[:, 0:KEYS[st]], ACT.Exp, bias=negmax[:, n % 2:n % 2 + 1],
                               accum_out=rowsum[:, n % 2:n % 2 + 1]).then_inc(s["exp_ready"], 1)

            def att_copy(l, st, n):
                act.wait_ge(s["pt_mm"], done("at", l, st, n))
                if n >= 2:
                    act.wait_ge(s["pv_mm"], done("av", l, st, n - 2))
                act.copy(probsT[st][:, n % 2, :], att_bank(st, n)[:, 0:KEYS[st]]).then_inc(s["pt_ready"], 1)

            def stage(grp, u):
                l, st = GROUPS[grp]
                if isinstance(u, int) and u < 2:
                    last = 1 if u == 0 else 2 * NT[st] - 1
                    act.wait_ge(s["key0_read"], done("ka", l, st, last))
                    act.wait_ge(s["key1_read"], done("kb", l, st, last))
                if not isinstance(u, int) or UNIT0[grp] + u:
                    act.wait_ge(s["idx_ready"], u + UNIT0[grp])
                act.copy(unit_cols[:, :], scores[st][:, bass.ds(u * 2 * N_KEYS, 2 * N_KEYS)]).then_inc(s["staged"], 1)

            def gexp(grp, u):
                act.wait_ge(s["best_ready"], u + UNIT0[grp] + 1)
                if not isinstance(u, int) or UNIT0[grp] + u:
                    act.wait_ge(s["w_ready"], u + UNIT0[grp])
                act.activation(gate_e[:], best[:], ACT.Exp, bias=gate_s[:, 1:2], accum_out=gate_s[:, 0:1]).then_inc(s["gexp_ready"], 1)

            def weigh(g):
                act.wait_ge(s["u_free"], g * TOPK + ROWS + TOPK)
                act.activation(acts[:], dots[:], ACT.Gelu_apprx_tanh).then_inc(s["gelu_ready"], 1)

            def add(grp, g, p):
                if p == 0:
                    act.wait_ge(s["w_ready"], g + 1)
                for k in range(PER_PIECE * p, PER_PIECE * (p + 1)):
                    act.wait_ge(s["v_free"], g * TOPK + ROWS + k - 3)
                    act.activation(diag[:, k % 4, :], ident[:], ACT.Copy, scale=wts[:, k:k + 1]).then_inc(s["diag_ready"], 1)

            def close_tile(grp, tile):
                act.wait_ge(s["acc_mm"], latent_tile(grp, tile) + 1)
                act.copy(out_tok[L_], acc).then_inc(s["acc_read"], 1)

            act.wait_ge(s["first_loaded"], 32)
            act.activation(csil, csil, ACT.Silu).then_inc(s["silu_ready"], 1)
            for job in ORDER:
                kind, a, b, n = job
                if kind in jobs:
                    jobs[kind](a, b, n, psum[:, BANK[job], :])
                elif kind == "as":
                    if n < 2:
                        att_exp(a, b, n)
                elif kind == "at":
                    att_copy(a, b, n)
                    if n + 2 < ATT_UNITS[b]:
                        att_exp(a, b, n + 2)
                elif kind == "stage":
                    stage(a, b)
                elif kind == "gexp":
                    gexp(a, b)
                elif kind == "weigh":
                    weigh(UNIT0[a] + b)
                elif kind == "add":
                    if GROUPS[a][1] == L_:
                        add(a, UNIT0[a] + b, n)
                elif kind == "close":
                    if GROUPS[a][1] == L_:
                        close_tile(a, tile_of(a, b))
                elif kind == LOOP:
                    with act.Fori(b, n) as t:
                        for kind, u, m, p in loop_steps(a, t):
                            if kind == "stage":
                                stage(a, u)
                            elif kind == "gexp":
                                gexp(a, u)
                            elif kind == "weigh":
                                weigh(u + UNIT0[a])
                            elif kind == "add":
                                add(a, u + UNIT0[a], p)
                            elif kind == "close":
                                close_tile(a, t + GROUP_TILE0[a])
            for t in range(TILES):
                act.wait_ge(s["y_mm"], t + 1)
                if t >= 2:
                    act.wait_ge(y_stored[t % 2], 16 * (t // 2))
                act.copy(row(0, t % 2), psum_cols[:, t % 4 * 1024:t % 4 * 1024 + 1024]).then_inc(s["y_copied"], 1)

        @block.vector
        def _(dve):
            n_link = [0]

            def link(ins):
                n_link[0] += 1
                ins.then_inc(s["dve_link"], 1)
                dve.wait_ge(s["dve_link"], n_link[0])

            def rms(l, st, i, g):
                if NUMBER["rms", l, st, i] == 0:
                    dve.wait_ge(s["const_loaded"], 16 * CONST_LOADS)
                dve.wait_ge(s["rstd_ready"], done("rms", l, st, i))
                for k in range(KC):
                    dve.tensor_tensor(hT[st][:, k, :], xT[:, k, COLS[st]], rstd[:, 0:WIDTH[st]], ALU.mult).then_inc(s["xn_ready"], 1)

            def modT_(l, st, n, g):
                m = modTs[l % 2]
                if n == 0:
                    dve.wait_ge(s["small_loaded"], 16 * SMALL_LOADS * (l + 1))
                dve.wait_ge(s["modT_mm"], done("modT", l, st, n))
                dve.tensor_tensor(m[:, 4 * n:4 * n + 4, :], g[:, 0:8].rearrange("p (j s) -> p j s", s=2),
                                  par[:, S_ADAB + 4 * n:S_ADAB + 4 * n + 4].unsqueeze(2).broadcast_to([P, 4, 2]),
                                  ALU.add).then_inc(s["mod_ready"], 1)
                dve.wait_ge(s["mod_ready"], done("modT", l, st, n))
                if n in (3, 9):
                    sc, gain = (SC_M, S_GMIX) if n == 3 else (SC_F, S_GFFN)
                    for one in range(2):
                        ins = dve.scalar_tensor_tensor(out=m[:, sc:sc + KC, one], in0=m[:, sc:sc + KC, one], scalar=1.0,
                                                       in1=par[:, gain:gain + KC], op0=ALU.add, op1=ALU.mult)
                        if one == 0:
                            link(ins)
                    ins.then_inc(s["scale_ready"], 1)

            def sine_arg(l, st, i, g):
                ph = phase(l, st)
                dve.wait_ge(s["filt_mm"], 2 * ph + i + 1)
                a, r = sin_arg[st][0:HY_FFN, 0, :], sin_arg[st][0:HY_FFN, 1, :]
                fb, fr = ((S_FB1, S_FR1), (S_FB2, S_FR2))[i]
                if i:
                    dve.wait_ge(s["sin_ready"], 2 * ph + 1)
                link(dve.tensor_scalar(a, g[0:HY_FFN, 0:WIDTH[st]], par[0:HY_FFN, fb:fb + 1], par[0:HY_FFN, fr:fr + 1], ALU.add, ALU.mult))
                link(dve.tensor_scalar(r, a, 1.0 / TWO_PI, ROUND, ALU.mult, ALU.add))
                link(dve.tensor_scalar(r, r, -ROUND, None, ALU.add))
                for c in (PI_HI, PI_MID, PI_LO):
                    link(dve.scalar_tensor_tensor(out=a, in0=r, scalar=-c, in1=a, op0=ALU.mult, op1=ALU.add))
                dve.tensor_scalar(a, a, SIN_MAX, -SIN_MAX, ALU.min, ALU.max).then_inc(s["arg_ready"], 1)

            def f3(l, st, t, g):
                q = NUMBER["f3", l, st, t]
                dve.wait_ge(s["f3_mm"], q + 1)
                dve.wait_ge(s["env_ready"], q + 1)
                if t == TILE0[st]:
                    link(dve.memset(tmp[0:1, q % 2, HY_CH:], 0.0))
                if q:
                    dve.wait_ge(s["ab_ready"], q)
                h, ab = x1[:, 0:512], filt_ab[st][:, t - TILE0[st], :, :]
                link(dve.tensor_tensor(h, g, tmp[:, q % 2, :], ALU.mult))
                dve.tensor_tensor(ab[:, 0, :], h[:, 0:HY_CH], h[:, HY_CH:], ALU.add)
                dve.tensor_tensor(ab[:, 1, :], h[:, 0:HY_CH], h[:, HY_CH:], ALU.subtract).then_inc(s["ab_ready"], 1)

            def qk(l, st, n, g):
                dve.wait_ge(s["hsq_ready"], done("qk", l, st, n))
                col = S_KG if n == 0 else S_QG
                dve.tensor_scalar(qk_dst(st, n), g[:, 0:WIDTH[st]], par[:, col:col + 1], 1.0 if n == 0 else HEAD_DIM ** -0.5,
                                  ALU.mult, ALU.mult).then_inc(s["qg_ready"], 1)

            def hs(l, st, n, g):
                dve.wait_ge(s["hr_ready"], done("hs", l, st, n))
                dve.wait_ge(s["qg_ready"], done("qk", l, st, n))
                dve.tensor_tensor(qk_dst(st, n), qk_dst(st, n), tmp[:, n % 2, 0:WIDTH[st]], ALU.mult).then_inc(s["qn_ready"], 1)

            def rot(l, st, n, g):
                q, x = NUMBER["rot", l, st, n], qk_dst(st, n)
                dve.wait_ge(s["rot_mm"], q + 1)
                if q:
                    dve.wait_ge(s["rot_ready"], q)
                if n == 4:
                    dve.wait_ge(s["y_ready"], done("df", l, st, 0))
                link(dve.tensor_tensor(work, g, cos_sin[:, 1, :], ALU.mult))
                link(dve.tensor_tensor(x, x, cos_sin[:, 0, :], ALU.mult))
                dve.tensor_tensor(x, x, work, ALU.add).then_inc(s["rot_ready"], 1)

            def vt(l, st, t, g):
                if t == TILE0[st] + NT[st] - 1:
                    dve.wait_ge(s["sgr_ready"], phase(l, st) + 1)
                    for i in range(TILE0[st], TILE0[st] + NT[st]):
                        dve.scalar_tensor_tensor(out=sg_v[:, i, :], in0=sg_v[:, i, :], scalar=sg_rstd[:, i:i + 1],
                                                 in1=sg_gain, op0=ALU.mult, op1=ALU.mult).then_inc(s["sgn_ready"], 1)

            def ck(l, st, n, g):
                dve.wait_ge(s["ck_mm"], l + 1)
                dve.tensor_copy(kT[L_][:, 0:PAST], g[:, 0:P]).then_inc(s["ck_ready"], 1)

            def hy(l, st, i, g):
                ph, w = phase(l, st), WIDTH[st]
                if i == 0:
                    dve.wait_ge(s["sin_ready"], 2 * ph + 2)
                    for b in range(2):
                        dve.memset(raw[st][:, b, 0:1], 0.0)
                        m = dve.memset(raw[st][:, b, w + 1:w + 2], 0.0)
                    m.then_inc(s["pads_ready"], 1)
                dve.wait_ge(s["hy_read"], done("hy", l, st, i))
                cc, dst = HY_CHUNK[i], hy_dst(st, i)
                for tap, step in ((0, link), (2, lambda ins: ins.then_inc(s["hy_conv"], 1))):
                    step(dve.scalar_tensor_tensor(out=dst, in0=raw[st][:, i % 2, tap:tap + w],
                                                  scalar=par[:, S_CONVW + 6 * tap + cc:S_CONVW + 6 * tap + cc + 1],
                                                  in1=dst, op0=ALU.mult, op1=ALU.add))
                if i in (1, 3):
                    dve.wait_ge(s["hy_conv"], 6 * ph + i + 1)
                    dve.tensor_tensor(dst, dst, x1[:, 0:w], ALU.mult).then_inc(s["gu_ready"], 1)

            def sp_(l, st, j, g):
                q, w, nt = NUMBER["sp", l, st, j], WIDTH[st], NT[st]
                dve.wait_ge(s["sp_mm"], q + 1)
                dve.wait_ge(s["su_ready"], done("su", l, st, j))
                dve.wait_ge(s["gu_ready"], 2 * phase(l, st) + 2)
                if q:
                    dve.wait_ge(s["sp_ready"], q)
                link(dve.tensor_tensor(grid(x1[:, 0:w], nt), grid(g[:, 0:w], nt),
                                       sg_bias[:, j, :].unsqueeze(1).broadcast_to([P, nt, P]), ALU.add))
                x = mix[:, 6 + j, COLS[st]]
                dve.tensor_tensor(x, x, x1[:, 0:w], ALU.mult).then_inc(s["sp_ready"], 1)

            def df(l, st, c, g):
                q = NUMBER["df", l, st, c]
                dve.wait_ge(s["df_mm"], q + 1)
                dve.wait_ge(s["filt_ready"], done("hf", l, st, c))
                dve.wait_ge(s["sp_ready"], done("sp", l, st, 1))
                if q:
                    dve.wait_ge(s["y_ready"], q)
                H = filt[st][:, c - TILE0[st], :, :].rearrange("p r n -> p (r n)")
                link(dve.tensor_tensor(x1[:, 0:512], g, H, ALU.mult))
                if st == L_:
                    dve.wait_ge(s["rot_ready"], done("rot", l, st, 3 if c == 0 else 4))
                link(dve.tensor_tensor(work[:, 0:HY_CH], g[:, 0:HY_CH], H[:, HY_CH:], ALU.mult))
                link(dve.tensor_tensor(work[:, HY_CH:], g[:, HY_CH:], H[:, 0:HY_CH], ALU.mult))
                link(dve.tensor_tensor(H[:, 0:HY_CH], x1[:, 0:HY_CH], x1[:, HY_CH:512], ALU.subtract))
                dve.tensor_tensor(H[:, HY_CH:], work[:, 0:HY_CH], work[:, HY_CH:], ALU.add).then_inc(s["y_ready"], 1)

            def cv(l, st, j, g):
                q, w = NUMBER["cv", l, st, j], WIDTH[st]
                dve.wait_ge(s["cv_mm"], q + 1)
                if q:
                    dve.wait_ge(s["cv_ready"], q)
                link(dve.scalar_tensor_tensor(out=x1[:, 0:w], in0=gate_u[st][:, j, :], scalar=par[:, S_SKIP + j:S_SKIP + j + 1],
                                              in1=g[:, 0:w], op0=ALU.mult, op1=ALU.add))
                dve.tensor_tensor(mix[:, 4 + j, COLS[st]], x1[:, 0:w], x0[st][:, j, :], ALU.mult).then_inc(s["cv_ready"], 1)

            def wo(l, st, j, g):
                x = xT[:, j, COLS[st]]
                dve.wait_ge(s["wo_mm"], done("wo", l, st, j))
                dve.scalar_tensor_tensor(out=x, in0=g[:, 0:WIDTH[st]], scalar=modTs[l % 2][:, G_M + j, st:st + 1], in1=x,
                                         op0=ALU.mult, op1=ALU.add).then_inc(s["x_ready"], 1)

            def tok(l, st, i, g):
                dve.wait_ge(s["tok_mm"], done("tok", l, st, i))
                dve.tensor_copy(h_tok[st][:, i * 512:(i + 1) * 512], g).then_inc(s["tok_ready"], 1)

            def kb(l, st, i, g):
                dve.wait_ge(s["kb_mm"], done("kb", l, st, i))
                dve.tensor_copy(key_dst(st, i, 1), grid(g, 4)).then_inc(s["key1_read"], 1)

            jobs = {"rms": rms, "modT": modT_, "f1": lambda l, st, n, g: sine_arg(l, st, 0, g),
                    "f2": lambda l, st, n, g: sine_arg(l, st, 1, g), "f3": f3, "qk": qk, "hs": hs, "rot": rot, "vt": vt,
                    "ck": ck, "hy": hy, "sp": sp_, "df": df, "cv": cv, "wo": wo, "tok": tok, "kb": kb}

            def att_max(l, st, n):
                dve.wait_ge(s["sc_mm"], done("as", l, st, n))
                dve.tensor_reduce(negmax[:, n % 2:n % 2 + 1], att_bank(st, n)[:, 0:KEYS[st]], AX.X, ALU.max, negate=True
                                  ).then_inc(s["max_ready"], 1)

            def att_norm(l, st, n):
                dve.wait_ge(s["exp_ready"], done("as", l, st, n))
                link(dve.reciprocal(rinv[:, n % 2:n % 2 + 1], rowsum[:, n % 2:n % 2 + 1]))
                if n >= 2:
                    dve.wait_ge(s["pt_mm"], done("at", l, st, n - 2))
                dve.tensor_scalar(softmax_diag[:, n % 2, :], ident[:], rinv[:, n % 2:n % 2 + 1], None, ALU.mult
                                  ).then_inc(s["probs_ready"], 1)

            def att_out(l, st, n):
                if (n + 1) % (2 * NT[st]) == 0:
                    c = n // (2 * NT[st])
                    dve.wait_ge(s["pv_mm"], done("av", l, st, n))
                    dve.tensor_copy(mix[:, c, COLS[st]], out_bank(st, c)[:, 0:WIDTH[st]]).then_inc(s["attn_ready"], 1)

            def top16(vals, idxs, src, step):
                step(dve.max(vals[:, 0:8], src))
                step(dve.max_index(idxs[:, 0:8], vals[:, 0:8], src))
                step(dve.match_replace(src, vals[:, 0:8], src, -3.0e38))
                step(dve.max(vals[:, 8:16], src))
                step(dve.max_index(idxs[:, 8:16], vals[:, 8:16], src))

            def pick(grp, u, to, part):
                count = [PICK_LINKS[part]]
                v = u + UNIT0[grp]
                looped = not isinstance(u, int)

                def step(ins):
                    count[0] += 1
                    ins.then_inc(s["topk_link"], 1)
                    dve.wait_ge(s["topk_link"], v * TOPK_LINKS + count[0])
                    if looped and count[0] not in STEPS_BEFORE_PLAIN:
                        dve.sem_inc(s["dve_tick"], 1)

                square = [P, TOPK, TOPK]
                if part == 0:
                    dve.wait_ge(s["staged"], v + 1)
                    if looped:
                        dve.sem_inc(s["dve_tick"], 1)
                if part < 2:
                    top16(topv[:, part, :], topi[:, part, :], unit_s[:, part, :], step)
                elif part == 2:
                    if looped or v:
                        dve.wait_ge(s["gexp_ready"], v)
                    step(dve.tensor_tensor(grid(cand[:, :], TOPK), topv[:, 0, :].unsqueeze(2).broadcast_to(square),
                                           topv[:, 1, :].unsqueeze(1).broadcast_to(square), ALU.add))
                    top16(best[:], pos[:], cand[:, :], step)
                    dve.tensor_scalar(gate_s[:, 1:2], best[:, 0:1], -1.0, None, ALU.mult).then_inc(s["best_ready"], 1)
                elif part == 3:
                    step(dve.tensor_scalar(posij[:, 0, :], pos[:], 4, None, ALU.logical_shift_right))
                    step(dve.tensor_scalar(posij[:, 1, :], pos[:], TOPK - 1, None, ALU.bitwise_and))
                    step(dve.tensor_copy(posf, posij))
                    step(dve.tensor_copy(topf, topi))
                else:
                    half, oh = part - 4, grid(onehot[:, :], TOPK)
                    step(dve.tensor_tensor(oh, iota16.unsqueeze(1).broadcast_to(square),
                                           posf[:, half, :].unsqueeze(2).broadcast_to(square), ALU.is_equal))
                    step(dve.tensor_tensor(oh, oh, topf[:, half, :].unsqueeze(1).broadcast_to(square), ALU.mult))
                    step(dve.tensor_reduce(picked[:, half, :], oh, AX.X, ALU.add))
                if part == 5:
                    step(dve.scalar_tensor_tensor(out=idxf[:], in0=picked[:, 0, :], scalar=float(N_KEYS), in1=picked[:, 1, :],
                                                  op0=ALU.mult, op1=ALU.add))
                    dve.tensor_scalar(idx[to][:], idxf[:], float(GROUPS[grp][0] * N_EXPERTS), None, ALU.add).then_inc(s["idx_ready"], 1)
                assert count[0] == PICK_LINKS[part + 1], count

            def dot(grp, u, t, p):
                for k in range(PER_PIECE * p, PER_PIECE * (p + 1)):
                    dve.wait_ge(row_landed[0][k % ROWS], row_value(u + UNIT0[grp], k))
                    dve.scalar_tensor_tensor(out=row(0, k), in0=row(0, k), scalar=1.0,
                                             in1=h_tok[GROUPS[grp][1]][:, bass.ds(t * D_MODEL, D_MODEL)], op0=ALU.mult,
                                             op1=ALU.mult, accum_out=dots[:, k:k + 1]).then_inc(s["u_free"], 1)

            def add(g, u, p):
                for k in range(PER_PIECE * p, PER_PIECE * (p + 1)):
                    dve.wait_ge(row_landed[1][k % ROWS], row_value(g, k))
                    x = grid(row(1, k), KC)
                    if u == 0 and k == 0:
                        m = dve.tensor_scalar(out_tok[C_], x, wts[:, k:k + 1], None, ALU.mult)
                    else:
                        dve.wait_ge(s["v_free"], g * TOPK + k + ROWS)
                        m = dve.scalar_tensor_tensor(out=out_tok[C_], in0=x, scalar=wts[:, k:k + 1], in1=out_tok[C_],
                                                     op0=ALU.mult, op1=ALU.add)
                    m.then_inc(s["v_free"], 1)

            def weigh(grp, u):
                g = u + UNIT0[grp]
                dve.wait_ge(s["gexp_ready"], g + 1)
                dve.reciprocal(gate_s[:, 2:3], gate_s[:, 0:1]).then_inc(s["wlink"], 1)
                dve.wait_ge(s["wlink"], g + 1)
                dve.wait_ge(s["gelu_ready"], g + 1)
                dve.scalar_tensor_tensor(out=wts[:], in0=acts[:], scalar=gate_s[:, 2:3], in1=gate_e[:],
                                         op0=ALU.mult, op1=ALU.mult).then_inc(s["w_ready"], 1)
                dve.wait_ge(s["w_ready"], g + 1)

            def close_tile(grp, tile, t):
                l, st = GROUPS[grp]
                dve.wait_ge(s["back_mm"], tile + 1)
                for k in range(KC):
                    x = xT[:, k, bass.ds(t * P + COLS[st].start, P)]
                    m = dve.scalar_tensor_tensor(out=x, in0=acc8[:, k, :], scalar=modTs[l % 2][:, G_F + k, st:st + 1],
                                                 in1=x, op0=ALU.mult, op1=ALU.add)
                m.then_inc(s["x_added"], 1)

            dve.memset(zeros[:], 0.0).then_inc(s["zero_ready"], 1)
            for job in ORDER:
                kind, a, b, n = job
                if kind in jobs:
                    jobs[kind](a, b, n, psum[:, BANK[job], :])
                elif kind == "as":
                    att_max(a, b, n)
                    if n:
                        att_norm(a, b, n - 1)
                elif kind == "at":
                    if n == ATT_UNITS[b] - 2:
                        att_norm(a, b, n + 1)
                elif kind == "av":
                    att_out(a, b, n)
                elif kind == "pick":
                    pick(a, b, b % IDX_PLACES, n)
                elif kind == "dot":
                    dot(a, b, b // PEER_HEADS, n)
                elif kind == "add":
                    if GROUPS[a][1] == C_:
                        add(UNIT0[a] + b, b, n)
                elif kind == "weigh":
                    weigh(a, b)
                elif kind == "close":
                    close_tile(a, tile_of(a, b), b // PEER_HEADS)
                elif kind == LOOP:
                    with dve.Fori(b, n) as t:
                        for kind, u, m, p in loop_steps(a, t):
                            if kind == "pick":
                                pick(a, u, m % IDX_PLACES, p)
                            elif kind == "dot":
                                dot(a, u, t + (m // PEER_HEADS - 1), p)
                            elif kind == "weigh":
                                weigh(a, u)
                            elif kind == "close":
                                close_tile(a, t + GROUP_TILE0[a], t)


def _columns():
    def run(a, n=P):
        return list(range(a, a + n))

    hy0, sg0 = 768, 1536
    x0, x1, v = hy0, hy0 + HY_CH, hy0 + 2 * HY_CH
    q = [run(c * 64, 64) + run((c + 4) * 64, 64) for c in range(4)]
    return [run(512), run(640), run(sg0 + 256), run(sg0 + 384), run(x1), run(v), run(x1 + P), run(v + P),
            run(x0), run(x0 + P), run(sg0), run(sg0 + P), *q]


def _blocks(w, cols):
    l, r, _ = w.shape
    w = w[:, :, np.concatenate([np.asarray(c) for c in cols])].reshape(l, r // P, P, len(cols) // 2, 2, P)
    return np.ascontiguousarray(w.transpose(0, 3, 2, 4, 1, 5)).reshape(l, len(cols) // 2, P, BLOCK)


def _constants():
    f = np.float32
    c = np.zeros((5, P, P), f)
    c[0] = np.eye(P, dtype=f)
    c[1] = 1.0 / D_MODEL
    c[2] = np.kron(np.eye(2), np.full((64, 64), 1.0 / HEAD_DIM)).astype(f)
    i = np.arange(0, P, 2)
    c[3][i + 1, i], c[3][i, i + 1] = -1.0, 1.0
    time = [np.arange(n, dtype=f) / f(n - 1) for n in (LAT, CTX)]
    c[4][:, 0:TILES] = -np.concatenate(time).reshape(TILES, P).T
    c[4][:, TILES] = EPS
    c[4][:, TILES + 1:TILES + 1 + TOPK] = np.arange(TOPK)
    inv = f(ROPE_THETA) ** (-np.arange(HEAD_DIM // 4, dtype=f) / f(HEAD_DIM // 4))
    t = np.arange(LAT)
    ang = np.concatenate([(t // GRID_W).astype(f)[:, None] * inv, (t % GRID_W).astype(f)[:, None] * inv], -1)
    ang = ang[:, np.arange(P) % HEAD_DIM // 2].T
    rope = np.stack([np.cos(ang), np.sin(ang)], 1).astype(f)

    def waves(n):
        a = np.pi * (2 * np.arange(n)[None, :] + 1) * np.arange(n)[:, None] / (2 * n)
        return np.cos(a), np.sin(a)

    feats = []
    for n, tn in zip((LAT, CTX), time):
        w = f(2.0 * np.pi) * np.arange(n, dtype=f) / f(n)
        z = w[:, None] * np.linspace(1e-4, HY_BANDS - 1, HY_BANDS, dtype=f)[None, :]
        feats.append(np.concatenate([tn[:, None], np.cos(z), -np.sin(z)], -1))
    feats = np.ascontiguousarray(np.concatenate(feats).T.astype(f))
    co, si = waves(LAT)
    dft = np.stack([m.reshape(LAT // P, P, LAT).transpose(1, 0, 2).reshape(P, BLOCK)
                    for m in (co, si, co.T / LAT, si.T / LAT)]).astype(f)
    co, si = waves(CTX)
    dft_ctx = np.stack([co, si, co.T / CTX, si.T / CTX], 1).astype(f)
    return c, rope, feats, dft, dft_ctx


def kernel(**inputs):
    import concourse.bacc as _bacc
    from concourse.bass_utils import run_bass_kernel_spmd as _run

    x = {k: np.asarray(v) for k, v in inputs.items()}
    f = np.float32
    L = DEPTH
    consts, rope, feats, dft, dft_ctx = _constants()

    def byP(a):
        return a.reshape(L, -1, P).transpose(0, 2, 1)

    small = np.zeros((L, P, S_COLS), f)
    small[:, :, S_GMIX:S_GMIX + KC] = byP(x["norm_mix_g"])
    small[:, :, S_GFFN:S_GFFN + KC] = byP(x["norm_ffn_g"])
    small[:, :, S_ADAB:S_ADAB + 6 * KC] = byP(x["ada_b"])
    small[:, :, S_QG] = np.concatenate([x["q_norm_g"]] * 2, 1)
    small[:, :, S_KG] = np.concatenate([x["k_norm_g"]] * 2, 1)
    for tap in range(3):
        small[:, :, S_CONVW + 6 * tap:S_CONVW + 6 * tap + 6] = byP(x["hy_conv_w"][:, tap])
    small[:, :, S_CONVB:S_CONVB + 6] = byP(x["hy_conv_b"])
    for col, name in ((S_FR1, "hy_freq1"), (S_FB1, "hy_fb1"), (S_FR2, "hy_freq2"), (S_FB2, "hy_fb2")):
        small[:, 0:HY_FFN, col] = x[name]
    small[:, :, S_SKIP:S_SKIP + 2] = byP(x["hy_skip"])
    wide = np.zeros((L, P, SG_W + 2 * P), f)
    wide[:, :, 0:SG_W] = x["sg_norm_g"][:, None, :]
    wide[:, :, SG_W:] = np.repeat(x["sg_b"].reshape(L, 2, 2, P), 64, axis=2).transpose(0, 2, 1, 3).reshape(L, P, 2 * P)
    fw12 = np.zeros((L, HY_FFN, 2 * HY_FFN + 512), f)
    fw12[:, 0:HY_EMB, 0:HY_FFN] = x["hy_fw1"]
    fw12[:, :, HY_FFN:2 * HY_FFN] = x["hy_fw2"]
    fw12[:, :, 2 * HY_FFN:] = x["hy_fw3"]
    blocks128 = [range(a, a + P) for a in range(0, D_MODEL, P)]
    heads = np.concatenate([np.r_[c * 64:c * 64 + 64, (c + 4) * 64:(c + 4) * 64 + 64] for c in range(4)])
    rows = np.concatenate([heads, np.arange(512, D_MODEL)])
    ada = x["ada_w"].reshape(L, 2, 4, P, N_MOD_BLOCKS, 512).transpose(0, 4, 1, 3, 2, 5).reshape(L, 2 * N_MOD_BLOCKS, P, BLOCK)
    tokens = np.concatenate([x["x_sample"][0], x["x_prompt"][0]], 0)
    arrays = {
        "xT_in": tokens.T.reshape(KC, P, TOK).transpose(1, 0, 2),
        "cT_in": np.stack([x["c"][0], x["c_ctx"]], -1).reshape(KC, P, 2).transpose(1, 0, 2),
        "cache_k": x["cache_k"][0].reshape(L, PAST, 2 * HEAD_DIM), "cache_v": x["cache_v"][0].reshape(L, PAST, 2 * HEAD_DIM),
        "ada": ada, "win": _blocks(x["w_in"], _columns()), "wout": _blocks(x["w_out"][:, rows], blocks128),
        "wq": _blocks(x["peer_wq"], blocks128), "dft": dft, "dft_ctx": dft_ctx, "small": small, "wide": wide,
        "decays": np.broadcast_to(x["hy_decay"].reshape(L, 1, 512), (L, P, 512)), "fw12": fw12,
        "featsT": feats, "sgw": x["sg_w"].transpose(0, 3, 1, 2),
        "keysT": x["peer_keys"].transpose(0, 2, 4, 1, 3).reshape(L, P, PEER_HEADS, N_KEYS), "rope": rope, "consts": consts,
        "peer_u": x["peer_u"].reshape(L * N_EXPERTS, D_MODEL), "peer_v": x["peer_v"].reshape(L * N_EXPERTS, D_MODEL),
    }
    arrays = {f"in_{k}": np.ascontiguousarray(v) for k, v in arrays.items()}
    outs = {"y_prompt": [CTX, D_MODEL], "y_sample": [LAT, D_MODEL], "new_k": [L, CTX, P], "new_v": [L, CTX, P]}
    nc = _bacc.Bacc("TRN2", target_bir_lowering=False, num_devices=1)
    args = {k[3:]: nc.dram_tensor(k, a.shape, mybir.dt.from_np(a.dtype), kind="ExternalInput").ap() for k, a in arrays.items()}
    for k, shape in outs.items():
        args[k] = nc.dram_tensor(f"out_{k}", shape, F32, kind="ExternalOutput").ap()
    mixer_peer_kernel(nc, **args)
    r = _run(nc, [arrays], core_ids=[0]).results[0]
    cache = (1, L, CTX, 2, HEAD_DIM)
    return (r["out_y_prompt"].reshape(1, CTX, D_MODEL), r["out_y_sample"].reshape(1, LAT, D_MODEL),
            r["out_new_k"].reshape(cache), r["out_new_v"].reshape(cache))
```
